# Optimizing a Trainium2 kernel written in Bass

```python
import math
import jax, jax.numpy as jnp
from jax import lax
import numpy as np
import jax
import jax.numpy as jnp

D_MODEL = 2048
BATCH = 1
SEQ = 256
DEPTH = 1

CHUNK = 64
N_META = 16
Q_BLOCK = 128
N_BRANCH = 2
BRANCH_WIDTH = D_MODEL // 2
HD_A = 128
H_A = BRANCH_WIDTH // HD_A
KV_A = H_A // 2
ROT_A = HD_A // 4
H_IDX = D_MODEL // 128
D_IDX = 64
ROT_IDX = D_IDX // 4
TOPK_MAX = 256
DK_B = 128
H_B = BRANCH_WIDTH // DK_B
DV_B = BRANCH_WIDTH // H_B
ROPE_THETA = 500000.0
EPS = 1e-6
SPLIT_SIZES = (H_A * HD_A, KV_A * HD_A, KV_A * HD_A, BRANCH_WIDTH,
               H_IDX * D_IDX, D_IDX, H_IDX,
               H_B * DK_B, H_B * DK_B, H_B * DV_B, BRANCH_WIDTH,
               N_BRANCH * D_MODEL)
N_IN = sum(SPLIT_SIZES)


def rms_norm(x, gain):
    xf = x.astype(jnp.float32)
    y = xf * lax.rsqrt(jnp.mean(xf * xf, axis=-1, keepdims=True) + EPS)
    return (y * gain.astype(jnp.float32)).astype(x.dtype)

def rope_tables(pos, rot_dim):
    inv = jnp.power(ROPE_THETA, -jnp.arange(0, rot_dim, 2, dtype=jnp.float32) / rot_dim)
    ang = pos.astype(jnp.float32)[:, None] * inv[None, :]
    return jnp.cos(ang), jnp.sin(ang)

def apply_partial_rope(x, cos, sin):
    half = cos.shape[-1]
    xr = x[..., :2 * half].astype(jnp.float32)
    x1, x2 = xr[..., :half], xr[..., half:]
    c, s = cos[None, :, None, :], sin[None, :, None, :]
    rot = jnp.concatenate([x1 * c - x2 * s, x2 * c + x1 * s], axis=-1)
    return jnp.concatenate([rot.astype(x.dtype), x[..., 2 * half:]], axis=-1)

def dsa_attention(q, k, v, qi, ki, wi, chunk_ids, topk):
    B, T, H, d = q.shape
    G = k.shape[2]
    R = H // G
    nb = T // Q_BLOCK
    scale = d ** -0.5
    ki32 = ki.astype(jnp.float32)

    def block(i):
        s0 = i * Q_BLOCK
        qb = lax.dynamic_slice_in_dim(q, s0, Q_BLOCK, axis=1)
        qib = lax.dynamic_slice_in_dim(qi, s0, Q_BLOCK, axis=1).astype(jnp.float32)
        wib = lax.dynamic_slice_in_dim(wi, s0, Q_BLOCK, axis=1).astype(jnp.float32)
        cq = lax.dynamic_slice_in_dim(chunk_ids, s0, Q_BLOCK)
        admissible = chunk_ids[None, :] <= cq[:, None]
        idx_logits = jnp.einsum('bqhd,bsd->bqhs', qib, ki32)
        score = jnp.einsum('bqhs,bqh->bqs', jax.nn.relu(idx_logits), wib)
        score = jnp.where(admissible[None], score, -jnp.inf)
        _, sel = lax.top_k(score, topk)
        valid = chunk_ids[sel] <= cq[None, :, None]
        k_sel = jax.vmap(lambda kk, ii: kk[ii])(k, sel)
        v_sel = jax.vmap(lambda vv, ii: vv[ii])(v, sel)
        qg = qb.reshape(B, Q_BLOCK, G, R, d)
        logits = jnp.einsum('bqgrd,bqkgd->bqgrk', qg, k_sel).astype(jnp.float32) * scale
        logits = jnp.where(valid[:, :, None, None, :], logits, -jnp.inf)
        p = jax.nn.softmax(logits, axis=-1).astype(v.dtype)
        o = jnp.einsum('bqgrk,bqkgd->bqgrd', p, v_sel)
        return o.reshape(B, Q_BLOCK, H, d)

    o = lax.map(block, jnp.arange(nb))
    return o.transpose(1, 0, 2, 3, 4).reshape(B, T, H, d)

def hgrn2_chunkwise(q, k, v, log_f):
    B, T, H, dk = q.shape
    dv = v.shape[-1]
    n = T // CHUNK

    def to_chunks(a):
        return a.reshape(B, n, CHUNK, H, a.shape[-1]).transpose(1, 0, 2, 3, 4)

    causal = jnp.tril(jnp.ones((CHUNK, CHUNK), dtype=bool))[None, :, :, None, None]

    def step(S, inp):
        q_, k_, v_, g_ = inp
        b = jnp.cumsum(g_, axis=1)
        diff = b[:, :, None] - b[:, None, :]
        decay = jnp.exp(jnp.where(causal, diff, -jnp.inf))
        attn = jnp.einsum('bthd,bshd,btshd->bhts', q_, k_, decay)
        o_intra = jnp.einsum('bhts,bshv->bthv', attn, v_)
        o_inter = jnp.einsum('bthd,bhdv->bthv', q_ * jnp.exp(b), S)
        b_last = b[:, -1]
        k_dec = k_ * jnp.exp(b_last[:, None] - b)
        S_new = jnp.exp(b_last)[..., None] * S + jnp.einsum('bshd,bshv->bhdv', k_dec, v_)
        return S_new, o_intra + o_inter

    S0 = jnp.zeros((B, H, dk, dv), jnp.float32)
    _, o = lax.scan(step, S0, (to_chunks(q), to_chunks(k), to_chunks(v), to_chunks(log_f)))
    return o.transpose(1, 0, 2, 3, 4).reshape(B, T, H, dv)

def hybrid_layer(x, lb, norm_g, w_in, q_norm_g, k_norm_g, idx_k_norm_g, hgrn_out_norm_g,
                 w_branch, w_out, rope_a, rope_i, chunk_ids, topk):
    B, T, D = x.shape
    h = rms_norm(x, norm_g)
    proj = h @ w_in
    cuts = np.cumsum(SPLIT_SIZES)[:-1].tolist()
    (q_a, k_a, v_a, z_a, q_i, k_i, w_i,
     q_b, f_b, i_b, z_b, gates) = jnp.split(proj, cuts, axis=-1)

    q = apply_partial_rope(rms_norm(q_a.reshape(B, T, H_A, HD_A), q_norm_g), *rope_a)
    k = apply_partial_rope(rms_norm(k_a.reshape(B, T, KV_A, HD_A), k_norm_g), *rope_a)
    v = v_a.reshape(B, T, KV_A, HD_A)
    qi = apply_partial_rope(q_i.reshape(B, T, H_IDX, D_IDX), *rope_i)
    ki = apply_partial_rope(rms_norm(k_i, idx_k_norm_g)[:, :, None, :], *rope_i)[:, :, 0, :]
    wi = w_i * (H_IDX ** -0.5 * D_IDX ** -0.5)
    o_a = dsa_attention(q, k, v, qi, ki, wi, chunk_ids, topk)
    y_a = o_a.reshape(B, T, BRANCH_WIDTH) * jax.nn.silu(z_a)

    qb = jax.nn.silu(q_b.astype(jnp.float32)).reshape(B, T, H_B, DK_B)
    lbh = lb.reshape(H_B, DK_B)
    f = lbh + (1.0 - lbh) * jax.nn.sigmoid(f_b.astype(jnp.float32).reshape(B, T, H_B, DK_B))
    vb = i_b.astype(jnp.float32).reshape(B, T, H_B, DV_B)
    o_b = hgrn2_chunkwise(qb, 1.0 - f, vb, jnp.log(f)).astype(x.dtype)
    o_b = rms_norm(o_b, hgrn_out_norm_g)
    y_b = o_b.reshape(B, T, BRANCH_WIDTH) * jax.nn.silu(z_b)

    y = jnp.stack([y_a, y_b], axis=2)
    p = jnp.einsum('btnc,ncd->btnd', y, w_branch)
    g = jax.nn.sigmoid(gates.reshape(B, T, N_BRANCH, D))
    merged = jnp.sum(g * p, axis=2)
    return x + merged @ w_out

def first_inputs(seed: int = 0) -> dict:
    key = jax.random.key(seed)
    ks = jax.random.split(key, 12)
    f32 = jnp.float32
    D = D_MODEL
    return {
        "x": jax.random.normal(ks[0], (BATCH, SEQ, D), f32),
        "meta_tokens": jax.random.normal(ks[1], (N_META, D), f32),
        "hgrn_lb_logits": 0.1 * jax.random.normal(ks[2], (DEPTH + 1, H_B * DK_B), f32),
        "norm_g": 1.0 + 0.02 * jax.random.normal(ks[3], (DEPTH, D), f32),
        "w_in": jax.random.normal(ks[4], (DEPTH, D, N_IN), f32) * D ** -0.5,
        "q_norm_g": 1.0 + 0.02 * jax.random.normal(ks[5], (DEPTH, HD_A), f32),
        "k_norm_g": 1.0 + 0.02 * jax.random.normal(ks[6], (DEPTH, HD_A), f32),
        "idx_k_norm_g": 1.0 + 0.02 * jax.random.normal(ks[7], (DEPTH, D_IDX), f32),
        "hgrn_out_norm_g": 1.0 + 0.02 * jax.random.normal(ks[8], (DEPTH, DV_B), f32),
        "w_branch": jax.random.normal(ks[9], (DEPTH, N_BRANCH, BRANCH_WIDTH, D), f32) * BRANCH_WIDTH ** -0.5,
        "w_out": jax.random.normal(ks[10], (DEPTH, D, D), f32) * D ** -0.5,
    }

def first_block(x, meta_tokens, hgrn_lb_logits, norm_g, w_in, q_norm_g, k_norm_g, idx_k_norm_g,
              hgrn_out_norm_g, w_branch, w_out):
    B, S, D = x.shape
    T = S + N_META
    Tp = -(-T // Q_BLOCK) * Q_BLOCK
    meta = jnp.broadcast_to(meta_tokens.astype(x.dtype)[None], (B, N_META, D))
    h = jnp.concatenate([meta, x, jnp.zeros((B, Tp - T, D), x.dtype)], axis=1)

    pos = jnp.arange(Tp, dtype=jnp.int32)
    chunk_ids = jnp.where(pos < N_META, 0, 1 + (pos - N_META) // CHUNK).astype(jnp.int32)
    rope_a = rope_tables(pos, ROT_A)
    rope_i = rope_tables(pos, ROT_IDX)
    topk = min(TOPK_MAX, S // 4)

    lb_all = jnp.cumsum(jax.nn.softmax(hgrn_lb_logits.astype(jnp.float32), axis=0), axis=0)

    for l in range(DEPTH):
        h = hybrid_layer(h, lb_all[l], norm_g[l], w_in[l], q_norm_g[l], k_norm_g[l],
                         idx_k_norm_g[l], hgrn_out_norm_g[l], w_branch[l], w_out[l],
                         rope_a, rope_i, chunk_ids, topk)
    return h[:, N_META:N_META + S]


GRID_W = 64
CTX_LEN = 256
D_MIX = D_MODEL
HEAD_DIM = 128
NA_WIDTH = D_MIX // 2
NA_HEADS = NA_WIDTH // HEAD_DIM
NA_KH = 8
NA_KW = 16
FN_WIDTH = D_MIX // 4
FN_GROUPS = 4
FN_GROUP_DIM = FN_WIDTH // FN_GROUPS
HY_WIDTH = D_MIX - NA_WIDTH - FN_WIDTH
HY_ORDER = 2
HY_BANDS = 16
HY_EMB = 1 + 2 * HY_BANDS
HY_FILTER_HIDDEN = 64
HY_FAST_DECAY = 0.3
HY_SLOW_DECAY = 1.5
HY_TARGET = 1e-2
HY_MIN_DECAY = math.log(HY_TARGET) / HY_SLOW_DECAY
HY_MAX_DECAY = math.log(HY_TARGET) / HY_FAST_DECAY
CONV_W = 3
D_FF = 11 * D_MODEL // 4
D_IN = 3 * NA_WIDTH + FN_WIDTH + (HY_ORDER + 1) * HY_WIDTH
N_MOD = 6


def rmsnorm(x, g):
    xf = x.astype(jnp.float32)
    y = xf * lax.rsqrt(jnp.mean(xf * xf, axis=-1, keepdims=True) + EPS)
    return (y * g.astype(jnp.float32)).astype(x.dtype)

def modulate(h, shift, scale):
    return h * (1 + scale) + shift

def dwconv_centred(x, w, b):
    L = x.shape[1]
    pad = CONV_W // 2
    xp = jnp.pad(x, ((0, 0), (pad, pad), (0, 0)))
    return sum(xp[:, j:j + L] * w[j] for j in range(CONV_W)) + b

def heads(t):
    return t.reshape(*t.shape[:-1], NA_HEADS, HEAD_DIM)

def split_projection(p):
    o1, o2, o3 = NA_WIDTH, 2 * NA_WIDTH, 3 * NA_WIDTH
    o4 = o3 + FN_WIDTH
    return p[..., :o1], p[..., o1:o2], p[..., o2:o3], p[..., o3:o4], p[..., o4:]

def neighbourhood_attention(q, k, v, kc, vc, rpb):
    B, L, H, Dh = q.shape
    rows = L // GRID_W
    kh = min(NA_KH, rows)
    n_loc = kh * NA_KW
    scale = Dh ** -0.5
    col = np.arange(GRID_W)
    col_start = np.clip(col - NA_KW // 2, 0, GRID_W - NA_KW)
    col_idx = col_start[:, None] + np.arange(NA_KW)[None, :]
    dcol = col_idx - col[:, None] + (NA_KW - 1)
    rpb_cols = rpb[:, :, dcol]
    kg = k.reshape(B, rows, GRID_W, H, Dh)
    vg = v.reshape(B, rows, GRID_W, H, Dh)
    q_rows = q.reshape(B, rows, GRID_W, H, Dh).transpose(1, 0, 2, 3, 4)

    def row_block(args):
        r, q_r = args
        r0 = jnp.clip(r - kh // 2, 0, rows - kh)
        k_rows = lax.dynamic_slice_in_dim(kg, r0, kh, axis=1)
        v_rows = lax.dynamic_slice_in_dim(vg, r0, kh, axis=1)
        k_win = jnp.take(k_rows, col_idx, axis=2)
        v_win = jnp.take(v_rows, col_idx, axis=2)
        drow = r0 + jnp.arange(kh) - r + (NA_KH - 1)
        bias = jnp.take(rpb_cols, drow, axis=1).transpose(0, 2, 1, 3)
        s_loc = jnp.einsum("bqhd,biqjhd->bhqij", q_r, k_win).astype(jnp.float32) * scale
        s_loc = s_loc + bias.astype(jnp.float32)
        s_ctx = jnp.einsum("bqhd,bchd->bhqc", q_r, kc).astype(jnp.float32) * scale
        s = jnp.concatenate([s_loc.reshape(B, H, GRID_W, n_loc), s_ctx], axis=-1)
        p = jax.nn.softmax(s, axis=-1).astype(v.dtype)
        p_loc = p[..., :n_loc].reshape(B, H, GRID_W, kh, NA_KW)
        return (jnp.einsum("bhqij,biqjhd->bqhd", p_loc, v_win)
                + jnp.einsum("bhqc,bchd->bqhd", p[..., n_loc:], vc))

    out = lax.map(row_block, (jnp.arange(rows), q_rows))
    return out.transpose(1, 0, 2, 3, 4).reshape(B, L, H * Dh)

def context_attention(qc, kc, vc):
    B, Lc, H, Dh = qc.shape
    s = jnp.einsum("bqhd,bkhd->bhqk", qc, kc).astype(jnp.float32) * (Dh ** -0.5)
    p = jax.nn.softmax(s, axis=-1).astype(vc.dtype)
    return jnp.einsum("bhqk,bkhd->bqhd", p, vc).reshape(B, Lc, H * Dh)

def fourier_mix(f):
    B, L, _ = f.shape
    fg = f.astype(jnp.float32).reshape(B, L, FN_GROUPS, FN_GROUP_DIM)
    y = jnp.fft.fft2(fg, axes=(1, 3), norm="ortho").real
    return y.reshape(B, L, FN_WIDTH).astype(f.dtype)

def hyena_kernel_spectrum(L, w1, b1, w2, b2, w3, freq):
    pos = jnp.arange(L, dtype=jnp.float32)[:, None]
    t = pos / max(L - 1, 1)
    bands = jnp.linspace(1e-4, HY_BANDS - 1, HY_BANDS, dtype=jnp.float32)
    ang = bands * (2.0 * math.pi / L) * pos
    z = jnp.concatenate([t, jnp.cos(ang), -jnp.sin(ang)], axis=-1)
    hdn = jnp.sin(freq * (z @ w1 + b1))
    hdn = jnp.sin(freq * (hdn @ w2 + b2))
    h = (hdn @ w3).astype(jnp.float32).reshape(L, HY_ORDER, 2, HY_WIDTH)
    deltas = jnp.linspace(HY_MIN_DECAY, HY_MAX_DECAY, HY_WIDTH, dtype=jnp.float32)
    h = h * jnp.exp(-t * jnp.abs(deltas))[:, None, None, :]
    hf, hb = h[:, :, 0], h[:, :, 1]
    kernel = jnp.concatenate([hf, jnp.zeros_like(hf[:1]), hb[:0:-1]], axis=0)
    return jnp.fft.rfft(kernel, axis=0)

def long_conv(z, k_spec, bias):
    L = z.shape[1]
    zf = z.astype(jnp.float32)
    y = jnp.fft.irfft(jnp.fft.rfft(zf, n=2 * L, axis=1) * k_spec, n=2 * L, axis=1)[:, :L]
    return (y + zf * bias).astype(z.dtype)

def hyena_mix(u, conv_w, conv_b, k_spec, bias):
    u = dwconv_centred(u, conv_w, conv_b)
    v, x1, x2 = jnp.split(u, HY_ORDER + 1, axis=-1)
    z = x1 * long_conv(v, k_spec[:, 0], bias[0])
    return x2 * long_conv(z, k_spec[:, 1], bias[1])

def merge_groups(a, f, hy, g):
    o1, o2 = NA_WIDTH, NA_WIDTH + FN_WIDTH
    return jnp.concatenate([rmsnorm(a, g[:o1]), rmsnorm(f, g[o1:o2]), rmsnorm(hy, g[o2:])], axis=-1)

def conv_gated_mlp(h, w_up, conv_w, conv_b, w_down):
    gate, up = jnp.split(h @ w_up, 2, axis=-1)
    return (jax.nn.gelu(dwconv_centred(gate, conv_w, conv_b), approximate=True) * up) @ w_down

def second_inputs(seed: int = 0) -> dict:
    key = jax.random.key(seed)
    ks = jax.random.split(key, 26)

    def nrm(k, shape, s):
        return s * jax.random.normal(k, shape, dtype=jnp.float32)

    def gain(k, shape):
        return 1.0 + 0.02 * jax.random.normal(k, shape, dtype=jnp.float32)

    return {
        "x": nrm(ks[0], (BATCH, SEQ, D_MODEL), 1.0),
        "c": nrm(ks[1], (BATCH, D_MODEL), 1.0),
        "ctx": nrm(ks[2], (BATCH, CTX_LEN, D_MODEL), 1.0),
        "c_ctx": nrm(ks[3], (D_MODEL,), 1.0),
        "ada_w": nrm(ks[4], (DEPTH, D_MODEL, N_MOD * D_MODEL), 0.3 * D_MODEL ** -0.5),
        "ada_b": nrm(ks[5], (DEPTH, N_MOD * D_MODEL), 0.02),
        "norm1_g": gain(ks[6], (DEPTH, D_MODEL)),
        "norm2_g": gain(ks[7], (DEPTH, D_MODEL)),
        "w_in": nrm(ks[8], (DEPTH, D_MODEL, D_IN), D_MODEL ** -0.5),
        "na_rpb": nrm(ks[9], (DEPTH, NA_HEADS, 2 * NA_KH - 1, 2 * NA_KW - 1), 0.02),
        "hy_conv_w": nrm(ks[10], (DEPTH, CONV_W, (HY_ORDER + 1) * HY_WIDTH), CONV_W ** -0.5),
        "hy_conv_b": nrm(ks[11], (DEPTH, (HY_ORDER + 1) * HY_WIDTH), 0.02),
        "hy_w1": nrm(ks[12], (DEPTH, HY_EMB, HY_FILTER_HIDDEN), HY_EMB ** -0.5),
        "hy_b1": nrm(ks[13], (DEPTH, HY_FILTER_HIDDEN), 0.02),
        "hy_w2": nrm(ks[14], (DEPTH, HY_FILTER_HIDDEN, HY_FILTER_HIDDEN), HY_FILTER_HIDDEN ** -0.5),
        "hy_b2": nrm(ks[15], (DEPTH, HY_FILTER_HIDDEN), 0.02),
        "hy_w3": nrm(ks[16], (DEPTH, HY_FILTER_HIDDEN, HY_ORDER * 2 * HY_WIDTH), HY_FILTER_HIDDEN ** -0.5),
        "hy_freq": gain(ks[17], (DEPTH, HY_FILTER_HIDDEN)),
        "hy_bias": nrm(ks[18], (DEPTH, HY_ORDER, HY_WIDTH), 0.1),
        "mix_norm_g": gain(ks[19], (DEPTH, D_MIX)),
        "w_out": nrm(ks[20], (DEPTH, D_MIX, D_MODEL), D_MIX ** -0.5),
        "ffn_w_up": nrm(ks[21], (DEPTH, D_MODEL, 2 * D_FF), D_MODEL ** -0.5),
        "ffn_conv_w": nrm(ks[22], (DEPTH, CONV_W, D_FF), CONV_W ** -0.5),
        "ffn_conv_b": nrm(ks[23], (DEPTH, D_FF), 0.02),
        "ffn_w_down": nrm(ks[24], (DEPTH, D_FF, D_MODEL), D_FF ** -0.5),
        "final_norm_g": gain(ks[25], (D_MODEL,)),
    }

def second_block(x, c, ctx, c_ctx, ada_w, ada_b, norm1_g, norm2_g, w_in, na_rpb,
              hy_conv_w, hy_conv_b, hy_w1, hy_b1, hy_w2, hy_b2, hy_w3, hy_freq, hy_bias,
              mix_norm_g, w_out, ffn_w_up, ffn_conv_w, ffn_conv_b, ffn_w_down, final_norm_g):
    L = x.shape[1]
    Lc = ctx.shape[1]
    xc = ctx
    s_lat = jax.nn.silu(c)
    s_ctx = jax.nn.silu(c_ctx)
    for l in range(DEPTH):
        update_ctx = l < DEPTH - 1
        mod = (s_lat @ ada_w[l] + ada_b[l])[:, None, :]
        sh1, sc1, g1, sh2, sc2, g2 = jnp.split(mod, N_MOD, axis=-1)
        mod_c = s_ctx @ ada_w[l] + ada_b[l]
        csh1, csc1, cg1, csh2, csc2, cg2 = jnp.split(mod_c, N_MOD, axis=-1)
        filt = (hy_w1[l], hy_b1[l], hy_w2[l], hy_b2[l], hy_w3[l], hy_freq[l])

        h = modulate(rmsnorm(x, norm1_g[l]), sh1, sc1)
        hc = modulate(rmsnorm(xc, norm1_g[l]), csh1, csc1)
        q, k, v, f, hy = split_projection(h @ w_in[l])
        if update_ctx:
            qc, kc, vc, fc, hyc = split_projection(hc @ w_in[l])
        else:
            kc, vc = jnp.split(hc @ w_in[l][:, NA_WIDTH:3 * NA_WIDTH], 2, axis=-1)
        kc_h, vc_h = heads(kc), heads(vc)
        a = neighbourhood_attention(heads(q), heads(k), heads(v), kc_h, vc_h, na_rpb[l])
        y = merge_groups(a, fourier_mix(f),
                         hyena_mix(hy, hy_conv_w[l], hy_conv_b[l], hyena_kernel_spectrum(L, *filt), hy_bias[l]),
                         mix_norm_g[l])
        x = x + g1 * (y @ w_out[l])
        if update_ctx:
            ac = context_attention(heads(qc), kc_h, vc_h)
            yc = merge_groups(ac, fourier_mix(fc),
                              hyena_mix(hyc, hy_conv_w[l], hy_conv_b[l], hyena_kernel_spectrum(Lc, *filt), hy_bias[l]),
                              mix_norm_g[l])
            xc = xc + cg1 * (yc @ w_out[l])

        ffn = (ffn_w_up[l], ffn_conv_w[l], ffn_conv_b[l], ffn_w_down[l])
        x = x + g2 * conv_gated_mlp(modulate(rmsnorm(x, norm2_g[l]), sh2, sc2), *ffn)
        if update_ctx:
            xc = xc + cg2 * conv_gated_mlp(modulate(rmsnorm(xc, norm2_g[l]), csh2, csc2), *ffn)
    return rmsnorm(x, final_norm_g)


def setup_inputs(seed=0):
    out = dict(first_inputs(seed))
    for name, value in second_inputs(seed + 1).items():
        if name != "x":
            out[name + "_2"] = value
    return out


def reference(
    x, meta_tokens, hgrn_lb_logits, norm_g, w_in, q_norm_g, k_norm_g, idx_k_norm_g,
    hgrn_out_norm_g, w_branch, w_out, c_2, ctx_2, c_ctx_2, ada_w_2, ada_b_2, norm1_g_2,
    norm2_g_2, w_in_2, na_rpb_2, hy_conv_w_2, hy_conv_b_2, hy_w1_2, hy_b1_2, hy_w2_2, hy_b2_2,
    hy_w3_2, hy_freq_2, hy_bias_2, mix_norm_g_2, w_out_2, ffn_w_up_2, ffn_conv_w_2,
    ffn_conv_b_2, ffn_w_down_2, final_norm_g_2,
):
    x = first_block(
        x, meta_tokens, hgrn_lb_logits, norm_g, w_in, q_norm_g, k_norm_g, idx_k_norm_g,
        hgrn_out_norm_g, w_branch, w_out,
    )
    return second_block(
        x, c_2, ctx_2, c_ctx_2, ada_w_2, ada_b_2, norm1_g_2, norm2_g_2, w_in_2, na_rpb_2,
        hy_conv_w_2, hy_conv_b_2, hy_w1_2, hy_b1_2, hy_w2_2, hy_b2_2, hy_w3_2, hy_freq_2,
        hy_bias_2, mix_norm_g_2, w_out_2, ffn_w_up_2, ffn_conv_w_2, ffn_conv_b_2, ffn_w_down_2,
        final_norm_g_2,
    )


_drawn_inputs = setup_inputs


def setup_inputs(seed=0):
    import zlib

    import numpy as np

    out = dict(_drawn_inputs(seed))
    spreads = {}
    factors = {'hgrn_lb_logits': 8.0,
     'norm_g': 4.465,
     'q_norm_g': 8.0,
     'k_norm_g': 8.0,
     'idx_k_norm_g': 8.0,
     'hgrn_out_norm_g': 21.387,
     'norm1_g_2': 39.354,
     'norm2_g_2': 38.294,
     'na_rpb_2': 200.0,
     'hy_conv_b_2': 200.0,
     'hy_b1_2': 8.0,
     'hy_b2_2': 8.0,
     'hy_freq_2': 8.0,
     'hy_bias_2': 37.088,
     'mix_norm_g_2': 200.0,
     'ffn_conv_b_2': 54.655,
     'final_norm_g_2': 20.584}
    for name, (base, spread) in spreads.items():
        noise = np.random.default_rng([zlib.crc32(name.encode()), seed]).standard_normal(out[name].shape)
        drawn = base * np.exp(spread * noise) if base else spread * noise
        out[name] = jnp.asarray(drawn.astype(out[name].dtype))
    for name, factor in factors.items():
        out[name] = (out[name] * factor).astype(out[name].dtype)
    return out
```

```python
import concourse.bass as bass
from concourse import mybir
from contextlib import ExitStack
import numpy as np

D = 2048
KT = D // 128
SEQ = 256
META = 16
T = META + SEQ
TOPK = 64
EPS = 1e-6
NEG = -1e30
GONE = -3e38
UC = 256
UW = KT * UC
HW = UW // 2

C_QA, C_KA, C_VA, C_ZA, C_QI, C_KI = 0, 1024, 1536, 2048, 3072, 4096
C_WI, C_QB, C_FB, C_IB, C_ZB, C_G = 4160, 4176, 5200, 6224, 7248, 8272

V_ADAB, V_NG, V_N1 = 0, 96, 112
V_N2, V_C, V_CC, V_HCW, V_HCB, V_MIX = 128, 144, 160, 176, 212, 224
V_QN, V_KN, V_ON, V_LB, V_FCB, V_FCW2 = 240, 241, 242, 243, 259, 303
V_FCW0, V_FCW1, V_END = 347, 391, 435
VEC_TILES = [(0, 128), (128, 112), (240, 107), (347, 88)]

PHASES = [("A", "Tx", 12), ("K", "K", 1), ("B", "Tall", 6), ("C", "N3", 6),
          ("D0", "Tx", 8), ("D1", "Tx", 8), ("D2", "Tx", 8),
          ("E", "BR", 8), ("F", "N2", 8),
          ("G", "T", 4), ("H", "N2", 4), ("I1", "T", 8), ("I2", "T", 8), ("J", "N2", 4), ("O", "N2", 8),
          ("L", "T", 44), ("M0", "DN", 11), ("M1", "DN", 11)]
U0, KIND, NUNITS = {}, {}, 0
UKIND = []
for _n, _k, _c in PHASES:
    U0[_n] = NUNITS
    KIND[_n] = _k
    NUNITS += _c
    UKIND += [_k] * _c
NU = {n: c for n, _, c in PHASES}
DMAS = [3 if k == "K" else 1 for k in UKIND]
LOADS = [sum(DMAS[v] for v in range(u % 2, u + 1, 2)) for u in range(NUNITS)]


FF = 5632
SECTIONS = 6
SH1, SC1, G1, SH2, SC2, G2 = range(SECTIONS)


def evacuated(u, p):
    return (u - p) // 2 + 1 if u >= p else 0


def program(nc, A, out):
    F32, F32R, I32 = mybir.dt.float32, mybir.dt.float32r, mybir.dt.int32
    ACT = mybir.ActivationFunctionType
    ALU = mybir.AluOpType
    AX = mybir.AxisListType.X
    ctx = ExitStack()
    with ctx:
        def sb(name, shape, dt=F32):
            return ctx.enter_context(nc.sbuf_tensor(name, shape, dt))
        sems = {}

        def S(name):
            if name not in sems:
                sems[name] = ctx.enter_context(nc.semaphore(name))
            return sems[name]

        raw = [sb(f"raw{i}", [128, UW]) for i in range(2)]
        whi = [sb(f"whi{i}", [128, HW], F32R) for i in range(2)]
        wlo = [sb(f"wlo{i}", [128, HW], F32R) for i in range(2)]
        phi = sb("phi", [128, KT, T], F32R)
        plo = sb("plo", [128, KT, T], F32R)
        ada = sb("ada", [128, 8192])
        arena = sb("arena", [128, 21300])
        ident = sb("ident", [128, 128])
        mean1 = sb("mean1", [128, 128])
        cols = sb("cols", [128, V_END])
        idxk = sb("idxk", [128, 1])
        ptmp = sb("ptmp", [128, 2, T])
        stat = sb("stat", [128, 64])
        small = sb("small", [128, 128])
        modL = sb("modL", [128, 96])
        modC = sb("modC", [128, 32])
        gains = sb("gains", [128, 48])
        silc = sb("silc", [128, 32])
        ps = [ctx.enter_context(nc.psum_tensor(f"ps{i}", [128, 512], F32)) for i in range(8)]

        def R(a, *shape):
            n = int(np.prod(shape))
            v = arena[:, a:a + n]
            return v.rearrange("p (a b) -> p a b", a=shape[0]) if len(shape) == 2 else v

        def RA(a, *shape):
            n = int(np.prod(shape))
            v = ada[:, a:a + n]
            return v.rearrange("p (a b) -> p a b", a=shape[0]) if len(shape) == 2 else v

        def rx(v, n):
            return v.rearrange("p (a b) -> p a b", a=n)

        xin = R(0, 3, D)
        vecs = R(6144, 4, 128)
        projA = R(0, 24 * 256)
        projB = R(6144, 12 * T)
        projC = R(9408, 3, 1536)
        oT = R(14016, 16 * 256)
        kiT = R(18112, T)
        wi = R(18384, 2, 16)
        selb = R(18416, 2, T)
        perm = R(18960, 2, 128)
        rope = R(19216, 4, T)
        gz = R(0, 48 * 256)
        x1 = R(0, 2, D)
        ada_slot = [RA(0, D), RA(D, D)]
        acc = [RA(2 * D, D), RA(3 * D, D)]
        ACC = [0, 0, 0, 1, 0, 1]
        ctxr = R(8192, 2, D)
        scr2 = R(16384, D)
        kcT = R(12288, 8 * 256)
        vc = R(14336, 2, 1024)
        xs1 = R(4096, 2, D)
        fhT = R(4096, 16 * 256)
        qkT = R(4096, 16 * 256)
        v2 = R(8192, 2, 1024)
        kF = R(8192, 2, 512)
        kG = R(9216, 4, 256)
        w3 = R(10240, D)
        y2a = R(16384, 2, 1024)
        win = R(16384, 2, 512)
        kCS = R(17408, 4, 256)
        y2fh = R(18432, 2, 1024)
        kz = R(20480, 260)
        kcd = R(20740, 256)
        hid = R(21000, 256)
        hyT = R(5120, 12 * 256)
        hfil = R(5120, 4, 512)
        Yt = R(5120, 4, 512)
        biasB = R(7168, 2, 512)
        u_tok = RA(0, 2, 1536)
        Ksp = RA(3072, 5, 512)
        AB = RA(5632, 4, 512)
        cv = RA(5632, 2, 256)
        w12 = RA(4352, 128)
        hid0 = RA(4096, 256)
        t512 = RA(7680, 512)
        U = RA(0, 48, 64)
        Uraw = RA(3072, 48, 64)
        flip = RA(6528, 128)
        L2, P2, PT2 = RA(3072, 2, 512), RA(4096, 2, 512), RA(5120, 2, 512)
        kcol = RA(6144, 64)
        diag = RA(6272, 2, 128)
        g1b = R(4096, D)
        xs2 = RA(0, 2, D)
        g2b, fgb = R(16384, D), R(18432, D)
        actT = R(4096, 44 * 256)
        cgt = R(15360, 2, 256)

        w_in = A["w_in"].rearrange("l (kt p) n -> p (l kt) n", p=128)
        w_br = A["w_branch"].rearrange("l b (kt p) n -> p (l b kt) n", p=128)
        w_o = A["w_out"].rearrange("l (kt p) n -> p (l kt) n", p=128)

        def wview(kind, buf, h):
            v = buf[:, :].rearrange("p (kt n) -> p kt n", n=UC)
            if kind == "K":
                return v[:, :, 0:128] if h == 0 else v[:, :, 128:144]
            if kind in ("Tx", "Tall", "BR", "T"):
                return v[:, :, 128 * h:128 * h + 128]
            return buf[:, HW * h:HW * h + HW]

        w_ada = A["ada_w_2"].rearrange("l (kt p) n -> p (l kt) n", p=128)
        w_in2 = A["w_in_2"].rearrange("l (kt p) n -> p (l kt) n", p=128)
        w_o2 = A["w_out_2"].rearrange("l (kt p) n -> p (l kt) n", p=128)
        w_up = A["ffn_w_up_2"].rearrange("l (kt p) n -> p (l kt) n", p=128)
        w_dn = A["ffn_w_down_2"].rearrange("l (kt p) n -> p (l kt) n", p=128)

        def sview(kind, buf, h):
            if kind == "K" and h == 1:
                return buf[:, 0:256].rearrange("p (kt n) -> p kt n", n=16)
            if kind in ("Tx", "Tall", "BR", "K", "T"):
                return buf[:, :].rearrange("p (kt n) -> p kt n", n=128)
            return buf[:, :]

        def halfof(base):
            return base // 2

        def units(eng, n, body):
            if n >= 4:
                with eng.Fori(0, n // 2) as j:
                    for i in range(2):
                        body(j * 2, i)
                if n % 2:
                    body(n - 1, 0)
            else:
                for i in range(n):
                    body(0, i)

        def stream(eng, split, name, evac, last=False):
            u0, n = U0[name], NU[name]

            def step(base, i):
                split(u0, base, i + 1, KIND[name])
                evac(base, i)
            m = n - 1
            if m >= 4:
                with eng.Fori(0, m // 2) as j:
                    for i in range(2):
                        step(j * 2, i)
                if m % 2:
                    step(m - 1, 0)
            else:
                for k in range(m):
                    step(0, k)
            if not last:
                split(u0 + n, 0, 0, UKIND[u0 + n])
            evac(n - 1 - (n - 1) % 2, (n - 1) % 2)

        def wait_evacs(eng, u):
            for p in range(2):
                eng.wait_ge(S(f"gemm_free{p}"), evacuated(u, p))

        NQ = [(projB, 0, T, 1), (projB, T, T, 1), (projB, 2 * T, T, 1), (projB, 3 * T, T, 1), (kiT, 0, T, 3)] + \
             [(projA, 2048 + 512 * i, 512, 2) for i in range(4)] + [(projA, 512 * i, 512, 0) for i in range(4)]
        NNORM = 9

        def rope_of(c):
            buf, a, w, kind = NQ[c]
            chunk = buf[:, a:a + w]
            b = 2 if kind in (0, 3) else 0
            if w == T:
                cs = [rope[:, b + i, :] for i in range(2)]
                sh = chunk
            else:
                cs = [rope[:, b + i, META:T].unsqueeze(1).to_broadcast([128, 2, 256]) for i in range(2)]
                sh = rx(chunk, 2)
            gain = {1: cols[:, V_KN:V_KN + 1], 2: cols[:, V_QN:V_QN + 1], 3: idxk[:, 0:1], 0: None}[kind]
            return chunk, w, sh, cs, gain, perm[:, 1 if kind in (0, 3) else 0, :]

        block = ctx.enter_context(nc.Block())

        @block.sync
        def _(sp):
            sp.dma_start(xin[:, 1:3, :], A["x"].rearrange("b (t p) n -> p (b t) n", p=128)).then_inc(S("x_in"), 16)
            sp.dma_start(xin[0:META, 0, :], A["meta_tokens"]).then_inc(S("x_in"), 16)
            sp.dma_start(ident[:, :], A["k_id"]).then_inc(S("id_in"), 16)
            for name, c0, n in (("norm_g", V_NG, 16), ("q_norm_g", V_QN, 1), ("k_norm_g", V_KN, 1),
                                ("hgrn_out_norm_g", V_ON, 1), ("hgrn_lb_logits", V_LB, 16),
                                ("ada_b_2", V_ADAB, 96), ("norm1_g_2", V_N1, 16), ("norm2_g_2", V_N2, 16),
                                ("c_2", V_C, 16), ("hy_conv_w_2", V_HCW, 36), ("hy_conv_b_2", V_HCB, 12),
                                ("mix_norm_g_2", V_MIX, 16), ("ffn_conv_b_2", V_FCB, 44)):
                a = A[name]
                v = a.rearrange({2: "a (t q) -> (a t) q", 3: "a b (t q) -> (a b t) q"}[len(a.shape)], q=128)
                t, r = [(i, c0 - f) for i, (f, rows) in enumerate(VEC_TILES) if f <= c0 < f + rows][0]
                sp.dma_start(vecs[r:r + n, t, :], v).then_inc(S("vec_in"), 16)
            sp.dma_start(vecs[V_CC - 128:V_CC - 112, 1, :], A["c_ctx_2"].rearrange("(t q) -> t q", q=128)).then_inc(S("vec_in"), 16)
            fcw = A["ffn_conv_w_2"].rearrange("a b (t q) -> (a b) t q", q=128)
            sp.dma_start(vecs[V_FCW2 - 240:V_FCW2 - 196, 2, :], fcw[2]).then_inc(S("vec_in"), 16)
            sp.dma_start(vecs[0:88, 3, :], fcw[0:2].rearrange("a t q -> (a t) q")).then_inc(S("vec_in"), 16)
            for h in range(2):
                sp.dma_start(idxk[64 * h:64 * h + 64, 0:1], A["idx_k_norm_g"].rearrange("a q -> q a")).then_inc(S("idxk_in"), 16)

            def load(src, kind, u0, base, i, c):
                p = (u0 + i) % 2
                if u0 + i >= 2:
                    sp.wait_ge(S("split_lo"), base * 2 + 2 * (u0 + i) - 2)
                dst = raw[p][:, :].rearrange("p (kt n) -> p kt n", n=UC)
                sp.dma_start(dst, src[:, :, bass.ds(c, UC)]).then_inc(S(f"loaded{p}"), 16)

            for name, u, c0 in (("A", 0, C_QI), ("A", 4, C_QA), ("A", 8, C_QB)):
                if u == 0:
                    for i in range(4):
                        load(w_in, "Tx", 0, 0, i, c0 + UC * i)
                    sp.dma_start(perm, A["k_perm"]).then_inc(S("rope_in"), 16)
                    sp.dma_start(rope, A["k_rope"]).then_inc(S("rope_in"), 16)
                else:
                    units(sp, 4, lambda b, i: load(w_in, "Tx", u, b, i, b * UC + (c0 + UC * i)))
            u = U0["K"]
            sp.wait_ge(S("split_lo"), 2 * u - 2)
            kv = raw[u % 2][:, :].rearrange("p (kt n) -> p kt n", n=UC)
            for d, c, n in ((0, C_KI, 64), (64, C_KI, 64), (128, C_WI, 16)):
                sp.dma_start(kv[:, :, d:d + n], w_in[:, :, c:c + n]).then_inc(S(f"loaded{u % 2}"), 16)
            for u, n, c0 in ((U0["B"], 2, C_KA), (U0["B"] + 2, 4, C_FB), (U0["C"], 2, C_VA), (U0["C"] + 2, 4, C_IB)):
                units(sp, n, lambda b, i: load(w_in, "Tx", u, b, i, b * UC + (c0 + UC * i)))
                if u == U0["C"]:
                    adm = RA(0, 2, T)
                    sp.dma_start(adm, A["k_adm"]).then_inc(S("adm_in"), 16)

            def load_ada(sec, kt0, base, i):
                for a in range(2):
                    n0 = 16 * sec + kt0 + 2 * i + a
                    if n0 >= 2 or (isinstance(base, int) and base > 0):
                        sp.wait_ge(S("ada_acc"), base * 2 + n0)
                    sp.dma_start(ada_slot[a].unsqueeze(1), w_ada[:, bass.ds(base * 2 + (kt0 + 2 * i + a), 1), D * sec:D * sec + D])\
                        .then_inc(S(f"ada_in{a}"), 16)
            for i in range(2):
                load(w_in, "Tx", U0["D0"], 0, i, C_ZA + UC * i)
            sp.wait_ge(S("att_out"), 16)
            sp.dma_start(R(2176, 8 * 128).bitcast(I32), A["k_lvl"]).then_inc(S("hg_in"), 16)
            sp.dma_start(R(3200, T), A["k_rst"]).then_inc(S("hg_in"), 16)
            sp.wait_ge(S("hg_done"), 4)
            for i in range(6):
                load(w_in, "Tx", U0["D0"], 0, i + 2, (C_ZA if i + 2 < 4 else C_ZB - 4 * UC) + UC * (i + 2))
                load_ada(0, 0, 0, i)

            def phase(src, name, c0):
                units(sp, NU[name], lambda b, i: load(src, "", U0[name], b, i, b * UC + (c0 + UC * i)))

            def phase_ada(src, name, c0, sec, kt0=0):
                for i in range(2):
                    load(src, "", U0[name], 0, i, c0 + UC * i)
                    load_ada(*last[0], i)

                def one(b, i):
                    load(src, "", U0[name], b, i + 2, b * UC + (c0 + UC * (i + 2)))
                    load_ada(sec, kt0, b, i)
                n = NU[name] - 2
                if n >= 4:
                    units(sp, n, one)
                else:
                    for i in range(n):
                        one(0, i)
                last[0] = (sec, kt0, n)
            last = [(0, 0, 6)]
            phase_ada(w_in, "D1", C_G, 1)
            phase_ada(w_in, "D2", C_G + 2048, 2)
            phase_ada(w_br, "E", 0, 3)
            sp.wait_ge(S("y_done"), 4)
            sp.dma_start(x1, A["x"].rearrange("b (t p) n -> p (b t) n", p=128)).then_inc(S("x_again"), 16)
            phase_ada(w_o, "F", 0, 4)
            wait_evacs(sp, U0["E"] + 7)
            sp.dma_start(ctxr, A["ctx_2"].rearrange("b (t p) n -> p (b t) n", p=128)).then_inc(S("ctx_in"), 16)
            phase_ada(w_in2, "G", 1024, 5)
            phase_ada(w_in2, "H", 2048, 5, 8)
            for i in range(2):
                load(w_in2, "", U0["I1"], 0, i, 3072 + UC * i)
                load_ada(*last[0], i)
            sp.wait_ge(S("pl_tp"), 16 * 3)
            def row(v):
                return v.rearrange("a (b n) -> (a b) n", b=1)
            for dst, src in ((kF, A["k_F"]), (kG, A["k_G"]), (w3[0:64, :], A["hy_w3_2"].rearrange("a k n -> (a k) n")),
                             (win, A["k_win"]), (kCS, A["k_CS"]), (kz, A["k_z"]), (kcd, A["k_cd"]),
                             (w12[0:33, 0:64], A["hy_w1_2"].rearrange("a k n -> (a k) n")),
                             (w12[0:64, 64:128], A["hy_w2_2"].rearrange("a k n -> (a k) n")),
                             (small[0:64, 104:105], A["hy_b1_2"].rearrange("a q -> q a")),
                             (small[0:64, 105:106], A["hy_b2_2"].rearrange("a q -> q a")),
                             (small[0:64, 106:107], A["hy_freq_2"].rearrange("a q -> q a"))):
                sp.dma_start(dst, src).then_inc(S("fh_in"), 16)
            units(sp, 6, lambda b, i: load(w_in2, "", U0["I1"] + 2, b, i, b * UC + (3584 + UC * i)))
            for i in range(2):
                load(w_in2, "", U0["I2"], 0, i, UC * i)
            sp.wait_ge(S("hy_tp"), 12)
            sp.dma_start(biasB, A["hy_bias_2"].rearrange("a b n -> (a b) n").partition_broadcast(128)).then_inc(S("bias_in"), 16)
            sp.wait_ge(S("y2_normed"), 4)
            rpb = A["na_rpb_2"]
            for rq in range(2):
                for h in range(8):
                    src = bass.AP(rpb.tensor, h * 465 + (5 - rq) * 31 + 15 - 63, [[1, 64], [31, 6], [1, 64]])
                    sp.dma_start(Uraw[64 * rq:64 * rq + 64, 6 * h:6 * h + 6, :], src).then_inc(S("rpb_in"), 16)
            sp.dma_start(kcol, A["k_col"]).then_inc(S("rpb_in"), 16)
            sp.dma_start(flip, A["k_flip"]).then_inc(S("rpb_in"), 16)
            for i in range(2, 8):
                load(w_in2, "", U0["I2"], 0, i, UC * i)
            phase(w_in2, "J", 2048)
            phase(w_o2, "O", 0)

            def gate_up(b, i):
                load(w_up, "", U0["L"], b, i, b * 128 + (FF * i))
            units(sp, 44, gate_up)
            sp.wait_ge(S("pl_tp"), 16 * 4)
            sp.dma_start(fgb, A["final_norm_g_2"].partition_broadcast(128)).then_inc(S("fg_in"), 16)

            def down(name, c):
                def one(b, i):
                    p = (U0[name] + i) % 2
                    sp.wait_ge(S("split_lo"), b * 2 + 2 * (U0[name] + i) - 2)
                    sp.dma_start(rx(raw[p][:, :], 4), w_dn[:, bass.ds(b * 4 + 4 * i, 4), 1024 * c:1024 * c + 1024])\
                        .then_inc(S(f"loaded{p}"), 16)
                units(sp, 11, one)
            down("M0", 0)
            down("M1", 1)
            for t in range(2):
                sp.wait_ge(S("final"), t + 1)
                sp.dma_start(out.rearrange("b (t p) n -> t p (b n)", p=128)[t], x1[:, t, :]).then_inc(S("out"), 16)
            sp.wait_ge(S("out"), 32)

        @block.gpsimd
        def _(pool):
            nc.gpsimd.memset(mean1[:, :], 1.0 / 128).then_inc(S("mean1_set"), 1)
            pool.wait_ge(S("hg_done"), 4)
            for a in range(2):
                nc.gpsimd.memset(acc[a], 0.0).then_inc(S("acc_zero"), 1)
            for sec in range(4):
                pool.wait_ge(S("ada_red"), sec + 1)
                for a in ((0, 1) if sec < 2 else (ACC[sec],)):
                    nc.gpsimd.memset(acc[a], 0.0).then_inc(S("acc_zero"), 1)

        @block.scalar
        def _(act):
            own_n = {}

            def own(name):
                own_n[name] = own_n.get(name, 0) + 1
                act.wait_ge(S(name), own_n[name])

            n_chain = [0]

            def chain(ins):
                n_chain[0] += 1
                ins.then_inc(S("act_chain"), 1)
                act.wait_ge(S("act_chain"), n_chain[0])

            def hi(u0, base, i, kind):
                p = (u0 + i) % 2
                if kind == "DN":
                    act.wait_ge(S("mm_half"), base * 2 + max(2 * (u0 + i) - 2, 2 * U0["M0"]))
                    nc.scalar.activation(phi[:, 4 * p:4 * p + 4, 0:256], rx(actT[:, bass.ds(base * 1024 + 1024 * i, 1024)], 4), ACT.Copy)\
                        .then_inc(S("dn_hi"), 1)
                for h in range(2):
                    if h == 0:
                        act.wait_ge(S(f"loaded{p}"), base * 8 + 16 * LOADS[u0 + i])
                    if u0 + i >= 1:
                        act.wait_ge(S("mm_half"), base * 2 + (2 * (u0 + i) + h - 1))
                    nc.scalar.activation(sview(kind, whi[h], h), wview(kind, raw[p], h), ACT.Copy)\
                        .then_inc(S("split_hi"), 1)

            def rms(k, src, P, n=D, scr=RA(0, D)):
                scr = scr[:, 0:n]
                nc.scalar.activation(scr[0:P, :], src, ACT.Square, accum_out=stat[0:P, k:k + 1]).then_inc(S("act_chain"), 1)
                n_chain[0] += 1
                act.wait_ge(S("act_chain"), n_chain[0])
                nc.scalar.activation(stat[0:P, 20 + k:21 + k], stat[0:P, k:k + 1], ACT.Sqrt,
                                     scale=1.0 / n, bias=epsc[0:P, 0:1]).then_inc(S("rms_root"), 1)
                own("rms_root")

            epsc = small[:, 0:1]

            def planes(s, mul, add, n):
                for kt in range(KT):
                    act.wait_ge(S("pl_tp"), 16 * s + kt + 1)
                    if 16 * s + kt >= 2:
                        act.wait_ge(S("pl_lo"), 16 * s + kt - 1)
                    if add is None:
                        i = nc.scalar.activation(ptmp[:, kt % 2, 0:n], ps[4 + kt % 4][:, 0:n], ACT.Copy, scale=mul(kt))
                    else:
                        i = nc.scalar.activation(ptmp[:, kt % 2, 0:n], ps[4 + kt % 4][:, 0:n], ACT.Identity, scale=mul(kt), bias=add(kt))
                    i.then_inc(S("pl_tmp"), 1)
                    own("pl_tmp")
                    act.wait_ge(S("pl_tmp"), 16 * s + kt + 1)
                    nc.scalar.activation(phi[:, kt, 0:n], ptmp[:, kt % 2, 0:n], ACT.Copy).then_inc(S("pl_hi"), 1)
                    own("pl_hi")

            def copy_planes(s, src, ready):
                for q in range(4):
                    ready(q)
                    nc.scalar.activation(phi[:, 4 * q:4 * q + 4, 0:256], rx(src[:, 1024 * q:1024 * q + 1024], 4), ACT.Copy)\
                        .then_inc(S("cp_hi"), 1)
                    own("cp_hi")

            act.wait_ge(S("eps_set"), 1)
            act.wait_ge(S("x_in"), 32)
            for t in range(3):
                rms(t, xin[0:META if t == 0 else 128, t, :], META if t == 0 else 128)
            for t, (c0, n) in enumerate(VEC_TILES):
                act.wait_ge(S("vec_tp"), t + 1)
                i = nc.scalar.activation(cols[:, c0:c0 + n], ps[4 + t][:, 0:n], ACT.Copy)
                i.then_inc(S("cols_set"), 1)
                own("cols_set")
            act.wait_ge(S("cols_set"), 4)
            nc.scalar.activation(silc[:, :], cols[:, V_C:V_C + 32], ACT.Silu).then_inc(S("silc_set"), 1)
            planes(0, lambda kt: cols[:, V_NG + kt:V_NG + kt + 1], None, T)

            def ev_T(dst, name, n, dst0=0):
                def f(base, i):
                    p = (U0[name] + i) % 2
                    for h in range(2):
                        act.wait_ge(S("mm_half"), base * 2 + (2 * (U0[name] + i) + h + 1))
                        c = nc.scalar.activation(dst[:, bass.ds(base * (2 * n) + (dst0 + (2 * i + h) * n), n)],
                                                 ps[2 * p + h][:, 0:n], ACT.Copy)
                    c.then_inc(S(f"gemm_free{p}"), 1)
                return f

            def ev_K(base, i):
                u = U0["K"]
                p = u % 2
                act.wait_ge(S("mm_half"), 2 * u + 1)
                nc.scalar.activation(kiT[:, :], ps[2 * p][:, 0:T], ACT.Copy)
                act.wait_ge(S("mm_half"), 2 * u + 2)
                nc.scalar.activation(wi[:, :, :], rx(ps[2 * p + 1][:, 0:32], 2), ACT.Copy, scale=16 ** -0.5 * 64 ** -0.5)\
                    .then_inc(S(f"gemm_free{p}"), 1)

            def ev_C(base, i):
                p = (U0["C"] + i) % 2
                act.wait_ge(S("mm_half"), base * 2 + (2 * (U0["C"] + i) + 2))
                nc.scalar.activation(projC[0:META, 0, bass.ds(base * UC + UC * i, UC)], ps[4 + p][0:META, 0:UC], ACT.Copy)
                nc.scalar.activation(projC[:, 1, bass.ds(base * UC + UC * i, UC)], ps[2 * p][:, 0:UC], ACT.Copy)
                nc.scalar.activation(projC[:, 2, bass.ds(base * UC + UC * i, UC)], ps[2 * p + 1][:, 0:UC], ACT.Copy)\
                    .then_inc(S(f"gemm_free{p}"), 1)

            hi(0, 0, 0, "Tx")
            act.wait_ge(S("pl_tp"), 16)
            stream(act, hi, "A", ev_T(projA, "A", 256))
            stream(act, hi, "K", ev_K)
            stream(act, hi, "B", ev_T(projB, "B", T))
            stream(act, hi, "C", ev_C)

            wait_evacs(act, U0["D0"] - 1)
            sq = RA(1024, 2, 512)
            rt = RA(2048, 2, 512)

            def square(c):
                chunk, w, *_ = rope_of(c)
                if c >= 2:
                    act.wait_ge(S("nk_mean"), c - 1)
                nc.scalar.activation(sq[:, c % 2, 0:w], chunk, ACT.Square).then_inc(S("nk_sq"), 1)
                own("nk_sq")
            square(0)
            for c in range(NNORM):
                if c + 1 < NNORM:
                    square(c + 1)
                w = rope_of(c)[1]
                act.wait_ge(S("nk_mean"), c + 1)
                if c >= 2:
                    act.wait_ge(S("nk_normed"), c - 1)
                nc.scalar.activation(rt[:, c % 2, 0:w], ps[4 + c % 2][:, 0:w], ACT.Sqrt, bias=epsc).then_inc(S("nk_root"), 1)
                own("nk_root")

            rl = RA(544, 2, T)
            act.wait_ge(S("nk_mean"), NNORM)
            for s in range(32):
                act.wait_ge(S("ix_mm"), s + 1)
                if s >= 2:
                    act.wait_ge(S("ix_acc"), s - 1)
                nc.scalar.activation(rl[:, s % 2, :], ps[4 + s % 4][:, 0:T], ACT.Relu).then_inc(S("ix_relu"), 1)
                own("ix_relu")

            P = RA(3072 + 544, 2, T)
            L = RA(3072, 2, T)
            PT = RA(4224, 2, 384)
            for a in range(16):
                act.wait_ge(S("at_max"), a + 1)
                if a >= 2:
                    act.wait_ge(S("at_tp"), a - 1)
                nc.scalar.activation(P[:, a % 2, :], L[:, a % 2, :], ACT.Exp, bias=small[:, 8 + a % 2:9 + a % 2],
                                     accum_out=small[:, 10 + a % 2:11 + a % 2]).then_inc(S("at_exp"), 1)
                own("at_exp")
                for b in ([a - 1] if a >= 1 else []) + ([a] if a == 15 else []):
                    act.wait_ge(S("at_tp"), b + 1)
                    if b >= 2:
                        act.wait_ge(S("at_pv"), b - 1)
                    nc.scalar.activation(PT[0:META, b % 2, 0:128], ps[6 + b % 2][0:META, 0:128], ACT.Copy)
                    nc.scalar.activation(PT[:, b % 2, 128:384], ps[6 + b % 2][:, 128:384], ACT.Copy).then_inc(S("at_pt"), 1)
                    own("at_pt")

            act.wait_ge(S("att_out"), 16)
            nc.scalar.activation(projA[:, 4096:6144], projA[:, 4096:6144], ACT.Silu).then_inc(S("hg_q"), 1)
            own("hg_q")
            f = projB[:, 4 * T:12 * T]
            nc.scalar.activation(f, f, ACT.Sigmoid).then_inc(S("hg_sig"), 1)
            own("hg_sig")
            act.wait_ge(S("lb_diff"), 1)
            nc.scalar.activation(small[:, 16:32], small[:, 16:32], ACT.Exp).then_inc(S("lb_exp"), 1)
            own("lb_exp")
            act.wait_ge(S("hg_f"), 1)
            nc.scalar.activation(R(0, 8 * T), f, ACT.Ln).then_inc(S("hg_ln"), 1)
            own("hg_ln")
            E = R(0, 2048)
            for l in range(7):
                act.wait_ge(S("lv_diff"), l + 1)
                nc.scalar.activation(E, E, ACT.Exp).then_inc(S("lv_exp"), 1)
                own("lv_exp")
            act.wait_ge(S("kd_diff"), 1)
            nc.scalar.activation(RA(2048, 8 * 144), RA(2048, 8 * 144), ACT.Exp, scale=-1.0).then_inc(S("kd_exp"), 1)
            own("kd_exp")
            nc.scalar.activation(E, RA(6144, 2048), ACT.Exp).then_inc(S("b_exp"), 1)
            own("b_exp")
            KDT = R(2176, 2, 256)
            for h in range(8):
                act.wait_ge(S("kd_tp"), h + 1)
                if h >= 2:
                    act.wait_ge(S("kd_mm"), h - 1)
                nc.scalar.activation(KDT[0:META, h % 2, 0:128], ps[4 + h % 2][0:META, 0:128], ACT.Copy)
                nc.scalar.activation(KDT[:, h % 2, 128:256], ps[4 + h % 2][:, 128:256], ACT.Copy).then_inc(S("kd_t"), 1)
                own("kd_t")
            for g in range(4):
                act.wait_ge(S("hg_mm"), 4 * g + 4)
                nc.scalar.activation(oT[:, 2048 + 512 * g:2560 + 512 * g], ps[4 + g][:, :], ACT.Copy).then_inc(S("hg_o"), 1)
                own("hg_o")
                act.wait_ge(S("hg_o"), g + 1)
                nc.scalar.activation(RA(512 * g, 512), oT[:, 2048 + 512 * g:2560 + 512 * g], ACT.Square).then_inc(S("hg_sq"), 1)
                own("hg_sq")
            for g in range(4):
                act.wait_ge(S("hg_mean"), g + 1)
                nc.scalar.activation(RA(2048 + 512 * g, 512), ps[4 + g][:, :], ACT.Sqrt, bias=epsc).then_inc(S("hg_root"), 1)
                own("hg_root")
            act.wait_ge(S("hg_done"), 4)

            for i, ph in enumerate(("D0", "D1", "D2")):
                stream(act, hi, ph, ev_T(gz, ph, 256, 4096 * i))
                wait_evacs(act, U0[ph] + 7)
                z = gz[:, 4096 * i:4096 * i + 4096]
                nc.scalar.activation(z, z, ACT.Silu if i == 0 else ACT.Sigmoid).then_inc(S("gz_act"), 1)
                own("gz_act")
            copy_planes(0, oT, lambda q: act.wait_ge(S("y_done"), q + 1))

            stream(act, hi, "E", lambda base, i: None)
            copy_planes(1, R(4096, 4096), lambda q: (wait_evacs(act, U0["E"] + 7), act.wait_ge(S("mm_half"), 2 * U0["F"])))
            nothing = lambda base, i: None
            stream(act, hi, "F", nothing)

            def ev_N(dst, name, dst0=0):
                def f(base, i):
                    p = (U0[name] + i) % 2
                    act.wait_ge(S("mm_half"), base * 2 + (2 * (U0[name] + i) + 2))
                    for t in range(2):
                        c = nc.scalar.activation(dst[:, t, bass.ds(base * UC + (dst0 + UC * i), UC)], ps[2 * p + t][:, 0:UC], ACT.Copy)
                    c.then_inc(S(f"gemm_free{p}"), 1)
                return f

            act.wait_ge(S("ctx_in"), 16)
            for t in range(2):
                rms(3 + t, ctxr[:, t, :], 128, D, scr2)
            act.wait_ge(S("gains_set"), 2)
            planes(1, lambda kt: gains[:, 16 + kt:17 + kt], lambda kt: modC[:, kt:kt + 1], 256)
            stream(act, hi, "G", ev_T(kcT, "G", 256))
            stream(act, hi, "H", ev_N(vc, "H"))

            wait_evacs(act, U0["F"] + 7)
            for t in range(2):
                rms(5 + t, x1[:, t, :], 128, D, scr2)
            planes(2, lambda kt: gains[:, kt:kt + 1], lambda kt: modL[:, kt:kt + 1], 256)
            stream(act, hi, "I1", ev_T(fhT, "I1", 256))

            wait_evacs(act, U0["I1"] + 7)
            for j in range(12):
                if j >= 2:
                    act.wait_ge(S("hy_tp"), j - 1)
                nc.scalar.activation(cv[:, j % 2, :], hyT[:, 256 * j:256 * j + 256], ACT.Identity,
                                     scale=cols[:, V_HCW + 12 + j:V_HCW + 13 + j], bias=cols[:, V_HCB + j:V_HCB + j + 1])\
                    .then_inc(S("cv_mid"), 1)
                own("cv_mid")
            act.wait_ge(S("hy_tp"), 12)
            for g in range(4):
                for t in range(2):
                    act.wait_ge(S("fd_mm"), 2 * g + t + 1)
                    nc.scalar.activation(AB[:, 2 * t:2 * t + 2, 128 * g:128 * g + 128], rx(ps[4 + (2 * g + t) % 4][:, 0:256], 2), ACT.Copy)\
                        .then_inc(S("fd_ab"), 1)
                    own("fd_ab")
            for t in range(2):
                act.wait_ge(S("fl_mm"), t + 1)
                nc.scalar.activation(y2fh[:, t, 0:512], ps[4 + t][:, :], ACT.Copy).then_inc(S("fl_out"), 1)
                own("fl_out")
                rms(7 + t, y2fh[:, t, 0:512], 128, 512, RA(3072, 512))
            for i, dst in enumerate((hid0, hid)):
                act.wait_ge(S("sin_arg"), i + 1)
                nc.scalar.activation(dst[0:64, :], hid[0:64, :] if i else hid0[0:64, :], ACT.Sin).then_inc(S("sin"), 1)
                own("sin")
            for t in range(2):
                act.wait_ge(S("hy_out"), t + 1)
                rms(9 + t, u_tok[:, t, 0:512], 128, 512, RA(5632, 512))

            stream(act, hi, "I2", ev_T(qkT, "I2", 256))
            stream(act, hi, "J", ev_N(v2, "J"))

            def pt2(b):
                act.wait_ge(S("na_tp"), b + 1)
                if b >= 2:
                    act.wait_ge(S("na_pv"), b - 1)
                nc.scalar.activation(PT2[:, b % 2, :], ps[6 + b % 2][:, :], ACT.Copy).then_inc(S("na_pt"), 1)
                own("na_pt")
            for a in range(16):
                act.wait_ge(S("na_max"), a + 1)
                if a >= 2:
                    act.wait_ge(S("na_tp"), a - 1)
                    act.wait_ge(S("na_inv"), a - 1)
                nc.scalar.activation(P2[:, a % 2, :], L2[:, a % 2, :], ACT.Exp, bias=small[:, 8 + a % 2:9 + a % 2],
                                     accum_out=small[:, 10 + a % 2:11 + a % 2]).then_inc(S("na_exp"), 1)
                own("na_exp")
                if a >= 1:
                    pt2(a - 1)
            pt2(15)
            act.wait_ge(S("na_out"), 16)

            def spread(k, dst):
                for q in range(4):
                    act.wait_ge(S("sp_mm"), 16 * k + 4 * q + 4)
                    nc.scalar.activation(dst[:, 512 * q:512 * q + 512], ps[4 + q][:, :], ACT.Copy).then_inc(S("spread"), 1)
                    own("spread")
            spread(0, g1b)
            for t in range(2):
                rms(11 + t, y2a[:, t, :], 128, 1024, RA(7168, 1024))
            planes(3, lambda kt: cols[:, V_MIX + kt:V_MIX + kt + 1], None, 256)
            stream(act, hi, "O", nothing)

            wait_evacs(act, U0["O"] + 7)
            for t in range(2):
                rms(13 + t, x1[:, t, :], 128, D, RA(4096, D))
            planes(4, lambda kt: gains[:, 32 + kt:33 + kt], lambda kt: modL[:, 16 * SH2 + kt:16 * SH2 + kt + 1], 256)
            spread(1, g2b)

            def ev_up(base, i):
                u0 = U0["L"]
                p = (u0 + i) % 2
                if i == 0:
                    for h in range(2):
                        act.wait_ge(S("mm_half"), base * 2 + (2 * (u0 + i) + h + 1))
                        act.wait_ge(S(f"gemm_free{(u0 + 1) % 2}"), halfof(base) + evacuated(u0 - 1, (u0 + 1) % 2))
                        nc.scalar.activation(cgt[:, h, :], ps[2 * p + h][:, 0:256], ACT.Identity,
                                             scale=cols[:, bass.ds(base + (V_FCW1 + h), 1)],
                                             bias=cols[:, bass.ds(base + (V_FCB + h), 1)]).then_inc(S("cg_mid"), 1)
                else:
                    act.wait_ge(S("cg_all"), base + 2)
                    nc.scalar.activation(cgt[:, :, :], cgt[:, :, :], ACT.Gelu_apprx_tanh).then_inc(S("gelu"), 1)
            stream(act, hi, "L", ev_up)
            stream(act, hi, "M0", nothing)
            stream(act, hi, "M1", nothing, last=True)
            for t in range(2):
                act.wait_ge(S("x3"), 4 * t + 4)
                rms(15 + t, x1[:, t, :], 128, D, RA(0, D))

        @block.vector
        def _(dve):
            own_n = {}

            def own(name):
                own_n[name] = own_n.get(name, 0) + 1
                dve.wait_ge(S(name), own_n[name])

            n_chain = [0]

            def chain(ins):
                n_chain[0] += 1
                ins.then_inc(S("dve_chain"), 1)
                dve.wait_ge(S("dve_chain"), n_chain[0])

            v = nc.vector
            v.memset(small[:, 1:2], 1.0).then_inc(S("ada_acc"), 1)
            v.memset(small[:, 0:1], EPS).then_inc(S("eps_set"), 1)
            own("eps_set")

            def lo(u0, base, i, kind):
                p = (u0 + i) % 2
                if kind == "DN":
                    dve.wait_ge(S("dn_hi"), base + (u0 + i - U0["M0"] + 1))
                    v.tensor_tensor(plo[:, 4 * p:4 * p + 4, 0:256], rx(actT[:, bass.ds(base * 1024 + 1024 * i, 1024)], 4),
                                    phi[:, 4 * p:4 * p + 4, 0:256].bitcast(F32), ALU.subtract).then_inc(S("dn_lo"), 1)
                for h in range(2):
                    dve.wait_ge(S("split_hi"), base * 2 + (2 * (u0 + i) + h + 1))
                    v.tensor_tensor(sview(kind, wlo[h], h), wview(kind, raw[p], h),
                                    sview(kind, whi[h], h).bitcast(F32), ALU.subtract).then_inc(S("split_lo"), 1)

            def normed(k, dst, src, P):
                dve.wait_ge(S("rms_root"), k + 1)
                chain(v.reciprocal(stat[0:P, 40 + k:41 + k], stat[0:P, 20 + k:21 + k]))
                v.tensor_scalar(dst, src, stat[0:P, 40 + k:41 + k], None, ALU.mult).then_inc(S("rows_normed"), 1)
                own("rows_normed")

            def planes(s, n):
                for kt in range(KT):
                    dve.wait_ge(S("pl_hi"), 16 * s + kt + 1)
                    v.tensor_tensor(plo[:, kt, 0:n], ptmp[:, kt % 2, 0:n], phi[:, kt, 0:n].bitcast(F32), ALU.subtract)\
                        .then_inc(S("pl_lo"), 1)
                    own("pl_lo")

            def copy_planes(s, src):
                for q in range(4):
                    dve.wait_ge(S("cp_hi"), 4 * s + q + 1)
                    v.tensor_tensor(plo[:, 4 * q:4 * q + 4, 0:256], rx(src[:, 1024 * q:1024 * q + 1024], 4),
                                    phi[:, 4 * q:4 * q + 4, 0:256].bitcast(F32), ALU.subtract).then_inc(S("cp_lo"), 1)
                    own("cp_lo")

            for t in range(3):
                n = META if t == 0 else 128
                normed(t, xin[0:n, t, :], xin[0:n, t, :], n)
            planes(0, T)
            none = lambda base, i: None
            lo(0, 0, 0, "Tx")
            for ph in ("A", "K", "B", "C"):
                stream(dve, lo, ph, none)

            wait_evacs(dve, U0["D0"] - 1)
            dve.wait_ge(S("rope_in"), 32)
            dve.wait_ge(S("idxk_in"), 32)
            rt = RA(2048, 2, 512)
            rr = RA(3072, 512)
            rot = RA(3584, 512)

            def turn(c):
                chunk, w, sh, (cs, sn), gain, _ = rope_of(c)
                dve.wait_ge(S("nk_rot"), c + 1)
                r = rot[:, 0:w] if w == T else rx(rot[:, 0:w], 2)
                p = ps[6 + c % 2][:, 0:w] if w == T else rx(ps[6 + c % 2][:, 0:w], 2)
                chain(v.tensor_tensor(r, p, sn, ALU.mult))
                chain(v.tensor_tensor(sh, sh, cs, ALU.mult))
                v.tensor_tensor(sh, sh, r, ALU.add).then_inc(S("nk_turned"), 1)
                own("nk_turned")
            for c in range(13):
                if c < NNORM:
                    chunk, w, sh, _, gain, _ = rope_of(c)
                    dve.wait_ge(S("nk_root"), c + 1)
                    chain(v.reciprocal(rr[:, 0:w], rt[:, c % 2, 0:w]))
                    v.scalar_tensor_tensor(chunk, chunk, gain, rr[:, 0:w], ALU.mult, ALU.mult).then_inc(S("nk_normed"), 1)
                    own("nk_normed")
                if c >= 1:
                    turn(c - 1)
            turn(12)

            dve.wait_ge(S("adm_in"), 16)
            adm = RA(0, 2, T)
            rl = RA(544, 2, T)
            sc = RA(2048, T)
            m8 = small[:, 32:40]
            for qt in range(2):
                for h in range(16):
                    s = qt * 16 + h
                    dve.wait_ge(S("ix_relu"), s + 1)
                    if s >= 1 and h >= 1:
                        dve.wait_ge(S("ix_acc"), s)
                    v.scalar_tensor_tensor(sc, rl[:, s % 2, :], wi[:, qt, h:h + 1], adm[:, qt, :] if h == 0 else sc,
                                           ALU.mult, ALU.add).then_inc(S("ix_acc"), 1)
                    own("ix_acc")
                dve.wait_ge(S("ix_acc"), 16 * qt + 16)
                for _r in range(TOPK // 8):
                    chain(v.max(m8, sc))
                    chain(v.match_replace(sc, m8, sc, GONE))
                v.tensor_scalar(selb[:, qt, :], sc, GONE / 1.5, NEG, ALU.is_gt, ALU.mult).then_inc(S("sel"), 1)
                own("sel")

            L = RA(3072, 2, T)
            P = RA(3072 + 544, 2, T)
            scale = 128 ** -0.5
            dve.wait_ge(S("sel"), 2)
            def att_out(a):
                qt, h = a // 8, a % 8
                dve.wait_ge(S("at_pv"), a + 1)
                v.tensor_copy(oT[:, 256 * h + 128 * qt:256 * h + 128 * qt + 128], ps[a % 2][:, 0:128]).then_inc(S("att_out"), 1)
                own("att_out")

            def logits(a):
                dve.wait_ge(S("at_qk"), a + 1)
                if a >= 2:
                    dve.wait_ge(S("at_exp"), a - 1)
                chain(v.scalar_tensor_tensor(L[:, a % 2, :], ps[4 + a % 2][:, 0:T], scale, selb[:, a // 8, :], ALU.mult, ALU.add))
                v.reduce_max(small[:, 8 + a % 2:9 + a % 2], L[:, a % 2, :], AX, negate=True).then_inc(S("at_max"), 1)
                own("at_max")

            def norm_p(a):
                dve.wait_ge(S("at_exp"), a + 1)
                chain(v.reciprocal(small[:, 12:13], small[:, 10 + a % 2:11 + a % 2]))
                v.tensor_scalar(P[:, a % 2, :], P[:, a % 2, :], small[:, 12:13], None, ALU.mult).then_inc(S("at_norm"), 1)
                own("at_norm")
            for a in range(16):
                logits(a)
                if a >= 1:
                    norm_p(a - 1)
                if a >= 3:
                    att_out(a - 3)
            norm_p(15)
            for a in (13, 14, 15):
                att_out(a)

            l0, l1 = cols[:, V_LB:V_LB + 8], cols[:, V_LB + 8:V_LB + 16]
            chain(v.tensor_tensor(small[:, 40:48], l0, l1, ALU.max))
            chain(v.tensor_tensor(small[:, 16:24], l0, small[:, 40:48], ALU.subtract))
            v.tensor_tensor(small[:, 24:32], l1, small[:, 40:48], ALU.subtract).then_inc(S("lb_diff"), 1)
            own("lb_diff")
            dve.wait_ge(S("lb_exp"), 1)
            chain(v.tensor_tensor(small[:, 40:48], small[:, 16:24], small[:, 24:32], ALU.add))
            chain(v.reciprocal(small[:, 48:56], small[:, 40:48]))
            chain(v.tensor_tensor(small[:, 56:64], small[:, 16:24], small[:, 48:56], ALU.mult))
            chain(v.tensor_scalar(small[:, 64:72], small[:, 56:64], -1.0, 1.0, ALU.mult, ALU.add))
            f = projB[:, 4 * T:12 * T]
            dve.wait_ge(S("hg_sig"), 1)
            for h in range(8):
                fh = f[:, T * h:T * h + T]
                i = v.tensor_scalar(fh, fh, small[:, 64 + h:65 + h], small[:, 56 + h:57 + h], ALU.mult, ALU.add)
            i.then_inc(S("hg_f"), 1)
            own("hg_f")
            G = R(0, 8, T)
            rst = R(3200, T)
            bx = RA(6144, 2048)
            bm = R(20310, 128)
            dve.wait_ge(S("hg_ln"), 1)
            dve.wait_ge(S("hg_in"), 32)
            chain(v.tensor_scalar(f, f, -1.0, 1.0, ALU.mult, ALU.add))
            for h in range(8):
                v.tensor_tensor_scan(bm[:, META * h:META * h + META], rst[:, 0:META], G[:, h, 0:META], 0.0, ALU.mult, ALU.add)
                i = v.tensor_tensor_scan(bx[:, 256 * h:256 * h + 256], rst[:, META:T], G[:, h, META:T], 0.0, ALU.mult, ALU.add)
            chain(i)
            q = projA[:, 4096:6144]
            kx = rx(f, 8)[:, :, META:T]
            Qt, Kt, attn = RA(0, 2048), RA(2048, 2048), RA(4096, 2048)
            E = R(0, 2048)
            lvl = R(2176, 8, 128).bitcast(I32)
            chain(v.memset(attn, 0.0))
            chain(v.memset(Qt, 0.0))
            chain(v.memset(Kt, 0.0))
            dve.wait_ge(S("hg_q"), 1)
            def halves(t, m):
                return t.rearrange("p (n two m) -> p n two m", two=2, m=m)

            def distances(l):
                m = 64 >> l
                bv, ev = halves(bx, m), halves(E, m)
                anc = bv[:, :, 0, m - 1:m].to_broadcast([128, 2048 // (2 * m), m])
                v.tensor_tensor(ev[:, :, 1, :], bv[:, :, 1, :], anc, ALU.subtract)
                v.tensor_tensor(ev[:, :, 0, :], anc, bv[:, :, 0, :], ALU.subtract).then_inc(S("lv_diff"), 1)
            distances(0)
            for l in range(8):
                if l < 7:
                    m = 64 >> l
                    dve.wait_ge(S("lv_exp"), l + 1)
                    if l >= 1:
                        dve.wait_ge(S("lv_mm"), 4 * l)
                    Kv = Kt.rearrange("p (h n two m) -> p h n two m", h=8, two=2, m=m)
                    kv = kx.rearrange("p h (n two m) -> p h n two m", two=2, m=m)
                    e4 = E.rearrange("p (h n two m) -> p h n two m", h=8, two=2, m=m)
                    v.tensor_tensor(halves(Qt, m)[:, :, 1, :], halves(q, m)[:, :, 1, :], halves(E, m)[:, :, 1, :], ALU.mult)
                    v.tensor_tensor(Kv[:, :, :, 0, :], kv[:, :, :, 0, :], e4[:, :, :, 0, :], ALU.mult).then_inc(S("lv_qk"), 1)
                    own("lv_qk")
                    if l < 6:
                        distances(l + 1)
                for g in range(4):
                    dve.wait_ge(S("lv_mm"), 4 * l + g + 1)
                    at = rx(attn[:, 512 * g:512 * g + 512], 4)
                    v.copy_predicated(at, lvl[:, l, :].unsqueeze(1).to_broadcast([128, 4, 128]), rx(ps[4 + g][:, :], 4))\
                        .then_inc(S("lv_sel"), 1)
                    if g == 3:
                        dve.wait_ge(S("lv_sel"), 4 * l + 4)
            KD = RA(2048, 8, 144)
            bm3, bx3 = rx(bm, 8), rx(bx, 8)
            dve.wait_ge(S("lv_mm"), 32)
            v.tensor_tensor(KD[:, :, 0:META], bm3, bm3[:, :, META - 1:META].to_broadcast([128, 8, META]), ALU.subtract)
            v.tensor_tensor(KD[:, :, META:144], bx3[:, :, 0:128], bx3[:, :, 127:128].to_broadcast([128, 8, 128]), ALU.subtract)\
                .then_inc(S("kd_diff"), 1)
            own("kd_diff")
            dve.wait_ge(S("kd_exp"), 1)
            v.tensor_tensor(KD, KD, rx(f, 8)[:, :, 0:144], ALU.mult).then_inc(S("kd"), 1)
            own("kd")
            dve.wait_ge(S("b_exp"), 1)
            v.tensor_tensor(Qt, q, E, ALU.mult).then_inc(S("q_in"), 1)
            own("q_in")
            S2 = R(2688, 8, 128)
            S1 = R(18960, 8, 128)
            dve.wait_ge(S("lv_sel"), 32)
            for h in range(8):
                dve.wait_ge(S("kd_mm"), h + 1)
                chain(v.tensor_copy(S1[:, h, :], ps[6 + h % 2][:, 0:128]))
                v.scalar_tensor_tensor(S2[:, h, :], S1[:, h, :], rx(E, 8)[:, h, 127:128], ps[6 + h % 2][:, 128:256],
                                       ALU.mult, ALU.add).then_inc(S("state"), 1)
                own("state")
            for g in range(4):
                dve.wait_ge(S("hg_root"), g + 1)
                w = slice(2048 + 512 * g, 2560 + 512 * g)
                chain(v.reciprocal(RA(4096 + 512 * g, 512), RA(2048 + 512 * g, 512)))
                v.scalar_tensor_tensor(oT[:, w], oT[:, w], cols[:, V_ON:V_ON + 1], RA(4096 + 512 * g, 512),
                                       ALU.mult, ALU.mult).then_inc(S("hg_done"), 1)
                own("hg_done")

            def ada_step(sec, kt0=0):
                def f(base, i):
                    for a in range(2):
                        n0 = 16 * sec + kt0 + 2 * i + a
                        k = base * 2 + (kt0 + 2 * i + a)
                        dve.wait_ge(S(f"ada_in{a}"), base * 16 + 16 * ((n0 - a) // 2 + 1))
                        dve.wait_ge(S("ada_acc"), base * 2 + (n0 + 1))
                        if sec < 2:
                            v.scalar_tensor_tensor(acc[1], ada_slot[a], silc[:, bass.ds(k + 16, 1)], acc[1], ALU.mult, ALU.add)
                        v.scalar_tensor_tensor(acc[ACC[sec]], ada_slot[a], silc[:, bass.ds(k, 1)], acc[ACC[sec]], ALU.mult, ALU.add)\
                            .then_inc(S("ada_acc"), 1)
                return f

            def both(f, g):
                def r(base, i):
                    f(base, i)
                    g(base, i)
                return r
            ZEROED = [2, 4, 6, 6, 7, 8]

            def modulation(sec):
                dve.wait_ge(S("ada_red"), sec + 1)
                w = slice(16 * sec, 16 * sec + 16)
                if sec < 2:
                    v.tensor_tensor(modC[:, w], ps[5][:, 0:16], cols[:, V_ADAB + 16 * sec:V_ADAB + 16 * sec + 16], ALU.add)
                v.tensor_tensor(modL[:, w], ps[4][:, 0:16], cols[:, V_ADAB + 16 * sec:V_ADAB + 16 * sec + 16], ALU.add)\
                    .then_inc(S("mod_set"), 1)
                own("mod_set")
            dve.wait_ge(S("silc_set"), 1)
            dve.wait_ge(S("acc_zero"), ZEROED[0])
            stream(dve, lo, "D0", ada_step(0))
            modulation(0)
            dve.wait_ge(S("acc_zero"), ZEROED[1])
            stream(dve, lo, "D1", ada_step(1))
            modulation(1)
            v.scalar_tensor_tensor(gains[:, 0:16], modL[:, 16:32], 1.0, cols[:, V_N1:V_N1 + 16], ALU.add, ALU.mult).then_inc(S("gains_set"), 1)
            own("gains_set")
            v.scalar_tensor_tensor(gains[:, 16:32], modC[:, 16:32], 1.0, cols[:, V_N1:V_N1 + 16], ALU.add, ALU.mult).then_inc(S("gains_set"), 1)
            own("gains_set")
            dve.wait_ge(S("acc_zero"), ZEROED[2])
            stream(dve, lo, "D2", ada_step(2))
            modulation(2)
            dve.wait_ge(S("acc_zero"), ZEROED[3])
            dve.wait_ge(S("gz_act"), 1)
            dve.wait_ge(S("hg_done"), 4)
            for c in range(4):
                w = slice(1024 * c, 1024 * c + 1024)
                v.tensor_tensor(oT[:, w], oT[:, w], gz[:, w], ALU.mult).then_inc(S("y_done"), 1)
                own("y_done")
            copy_planes(0, oT)
            dve.wait_ge(S("gz_act"), 3)

            def merge(base, i):
                p = (U0["E"] + i) % 2
                for h in range(2):
                    dve.wait_ge(S("mm_half"), base * 2 + (2 * (U0["E"] + i) + h + 1))
                    ga = gz[:, bass.ds(base * 512 + (4096 + 256 * (2 * i + h)), 256)]
                    gb = gz[:, bass.ds(base * 512 + (8192 + 256 * (2 * i + h)), 256)]
                    v.tensor_tensor(ga, ga, ps[2 * p + h][:, 0:256], ALU.mult)
                    v.tensor_tensor(gb, gb, ps[2 * p + h][:, 256:512], ALU.mult).then_inc(S("gated"), 1)
                    dve.wait_ge(S("gated"), base * 2 + (2 * i + h + 1))
                    m = v.tensor_tensor(ga, ga, gb, ALU.add)
                m.then_inc(S(f"gemm_free{p}"), 1)
            stream(dve, lo, "E", both(merge, ada_step(3)))
            modulation(3)
            dve.wait_ge(S("acc_zero"), ZEROED[4])
            wait_evacs(dve, U0["E"] + 7)
            copy_planes(1, R(4096, 4096))
            dve.wait_ge(S("x_again"), 16)

            def resid(base, i):
                p = (U0["F"] + i) % 2
                dve.wait_ge(S("mm_half"), base * 2 + (2 * (U0["F"] + i) + 2))
                for t in range(2):
                    c = x1[:, t, bass.ds(base * UC + UC * i, UC)]
                    m = v.tensor_tensor(c, c, ps[2 * p + t][:, 0:UC], ALU.add)
                m.then_inc(S(f"gemm_free{p}"), 1)
            stream(dve, lo, "F", both(resid, ada_step(4)))
            modulation(4)
            v.scalar_tensor_tensor(gains[:, 32:48], modL[:, 64:80], 1.0, cols[:, V_N2:V_N2 + 16], ALU.add, ALU.mult).then_inc(S("gains_set"), 1)
            own("gains_set")
            dve.wait_ge(S("acc_zero"), ZEROED[5])

            for t in range(2):
                normed(3 + t, ctxr[:, t, :], ctxr[:, t, :], 128)
            planes(1, 256)
            stream(dve, lo, "G", ada_step(5))
            stream(dve, lo, "H", ada_step(5, 8))
            modulation(5)

            for t in range(2):
                normed(5 + t, xs1[:, t, :], x1[:, t, :], 128)
            planes(2, 256)
            stream(dve, lo, "I1", none)
            for j in range(12):
                dve.wait_ge(S("cv_mid"), j + 1)
                x = hyT[:, 256 * j:256 * j + 256]
                c = cv[:, j % 2, :]
                chain(v.scalar_tensor_tensor(c[:, 1:256], x[:, 0:255], cols[:, V_HCW + j:V_HCW + j + 1], c[:, 1:256], ALU.mult, ALU.add))
                v.scalar_tensor_tensor(c[:, 0:255], x[:, 1:256], cols[:, V_HCW + 24 + j:V_HCW + 25 + j], c[:, 0:255], ALU.mult, ALU.add)\
                    .then_inc(S("cv_all"), 1)
                own("cv_all")
                if j >= 1:
                    dve.wait_ge(S("hy_tp"), j)
                    v.tensor_copy(u_tok[:, :, 128 * (j - 1):128 * j], rx(ps[4 + (j - 1) % 4][:, 0:256], 2)).then_inc(S("hy_tok"), 1)
                    own("hy_tok")
            dve.wait_ge(S("hy_tp"), 12)
            v.tensor_copy(u_tok[:, :, 128 * 11:128 * 12], rx(ps[7][:, 0:256], 2)).then_inc(S("hy_tok"), 1)
            own("hy_tok")
            for t in range(2):
                normed(7 + t, y2fh[:, t, 0:512], y2fh[:, t, 0:512], 128)
                v.memset(small[:, 107:108], 0.0).then_inc(S("y2_normed"), 1)
                own("y2_normed")
            MAGIC, TWO_PI_HI = 12582912.0, 6.28125
            for i, dst in enumerate((hid0, hid)):
                d = dst[0:64, :]
                n = t512[0:64, 0:256]
                dve.wait_ge(S("fm_mm"), i + 1)
                chain(v.tensor_scalar(d, ps[4 + i][0:64, 0:256], small[0:64, 104 + i:105 + i], small[0:64, 106:107], ALU.add, ALU.mult))
                chain(v.tensor_scalar(n, d, 1 / (2 * np.pi), MAGIC, ALU.mult, ALU.add))
                chain(v.tensor_scalar(n, n, MAGIC, None, ALU.subtract))
                chain(v.scalar_tensor_tensor(d, n, -TWO_PI_HI, d, ALU.mult, ALU.add))
                chain(v.scalar_tensor_tensor(d, n, -(2 * np.pi - TWO_PI_HI), d, ALU.mult, ALU.add))
                v.tensor_scalar(d, d, 3.1415925, -3.1415925, ALU.min, ALU.max).then_inc(S("sin_arg"), 1)
                own("sin_arg")
            dve.wait_ge(S("fh_in"), 16 * 12)
            for o in range(2):
                for t in range(2):
                    dve.wait_ge(S("fil_mm"), 2 * o + t + 1)
                    sm, df = hfil[:, t, :], hfil[:, 2 + t, :]
                    a, b = ps[4 + 2 * t], ps[5 + 2 * t]
                    chain(v.tensor_tensor(df, a[:, :], win[:, t, :], ALU.mult))
                    chain(v.scalar_tensor_tensor(t512, b[:, :], kz[:, 256 + t:257 + t], win[:, t, :], ALU.mult, ALU.mult))
                    chain(v.tensor_tensor(sm, df, t512, ALU.add))
                    v.tensor_tensor(df, df, t512, ALU.subtract).then_inc(S("fil"), 1)
                    own("fil")
                dve.wait_ge(S("ks_mm"), 2 * o + 1)
                for m in range(4):
                    chain(v.tensor_copy(Ksp[:, m, :], ps[4 + m][:, :]))
                chain(v.tensor_copy(Ksp[:, 4, :], ps[4][:, :]))
                v.memset(Ksp[0:1, 2, :], 0.0).then_inc(S("ksp"), 1)
                own("ksp")
                dve.wait_ge(S("ks_mm"), 2 * o + 2)
                v.tensor_copy(Ksp[0:1, 4, :], ps[4][0:1, :]).then_inc(S("ksp"), 1)
                own("ksp")
                for m in range(2):
                    dve.wait_ge(S("zs_mm"), o + 1)
                    C = Ksp[:, 4 if m == 0 else 1, :]
                    chain(v.tensor_tensor(Yt[:, m, :], ps[4 + m][:, :], Ksp[:, m, :], ALU.mult))
                    chain(v.tensor_tensor(t512, ps[6 + m][:, :], Ksp[:, 2 + m, :], ALU.mult))
                    chain(v.tensor_tensor(Yt[:, m, :], Yt[:, m, :], t512, ALU.subtract))
                    chain(v.tensor_tensor(Yt[:, 2 + m, :], ps[4 + m][:, :], Ksp[:, 2 + m, :], ALU.mult))
                    chain(v.tensor_tensor(t512, ps[6 + m][:, :], C, ALU.mult))
                    v.tensor_tensor(Yt[:, 2 + m, :], Yt[:, 2 + m, :], t512, ALU.add).then_inc(S("ys"), 1)
                    own("ys")
                dve.wait_ge(S("bias_in"), 16)
                for t in range(2):
                    dve.wait_ge(S("yt_mm"), 2 * o + t + 1)
                    z = u_tok[:, t, 0:512]
                    chain(v.tensor_tensor(t512, z, biasB[:, o, :], ALU.mult))
                    chain(v.tensor_tensor(t512, t512, ps[4 + t][:, :], ALU.add))
                    i = v.tensor_tensor(z, t512, u_tok[:, t, 512 * (o + 1):512 * (o + 2)], ALU.mult)
                    if o == 0:
                        i.then_inc(S("z1"), 1)
                        own("z1")
                    else:
                        i.then_inc(S("hy_out"), 1)
                        own("hy_out")
            for t in range(2):
                normed(9 + t, y2fh[:, t, 512:1024], u_tok[:, t, 0:512], 128)
                v.memset(small[:, 107:108], 0.0).then_inc(S("y2_normed"), 1)
                own("y2_normed")

            stream(dve, lo, "I2", none)
            stream(dve, lo, "J", none)
            dve.wait_ge(S("rpb_in"), 16 * 18)
            for c in range(6):
                dve.wait_ge(S("flipped"), c + 1)
                v.tensor_tensor(U[:, 8 * c:8 * c + 8, :], rx(ps[4 + c % 4][:, :], 8), kcol.unsqueeze(1).to_broadcast([128, 8, 64]), ALU.add)\
                    .then_inc(S("bias_set"), 1)
                own("bias_set")

            def na_logits(a):
                qt, h = a // 8, a % 8
                dve.wait_ge(S("na_qk"), a + 1)
                if a >= 2:
                    dve.wait_ge(S("na_exp"), a - 1)
                e0 = 6 * h + 2 - 2 * qt
                chain(v.scalar_tensor_tensor(rx(L2[:, a % 2, 0:256], 4), rx(ps[4 + a % 2][:, 0:256], 4), scale, U[:, e0:e0 + 4, :], ALU.mult, ALU.add))
                chain(v.tensor_scalar(L2[:, a % 2, 256:512], ps[4 + a % 2][:, 256:512], scale, None, ALU.mult))
                v.reduce_max(small[:, 8 + a % 2:9 + a % 2], L2[:, a % 2, :], AX, negate=True).then_inc(S("na_max"), 1)
                own("na_max")

            def na_inv(a):
                dve.wait_ge(S("na_exp"), a + 1)
                v.reciprocal(small[:, 96 + a % 4:97 + a % 4], small[:, 10 + a % 2:11 + a % 2]).then_inc(S("na_inv"), 1)
                own("na_inv")

            def na_out(a):
                qt, h = a // 8, a % 8
                dve.wait_ge(S("na_pv"), a + 1)
                v.tensor_scalar(y2a[:, qt, 128 * h:128 * h + 128], ps[a % 2][:, 0:128], small[:, 96 + a % 4:97 + a % 4], None, ALU.mult)\
                    .then_inc(S("na_out"), 1)
                own("na_out")
            for a in range(16):
                na_logits(a)
                if a >= 1:
                    na_inv(a - 1)
                if a >= 3:
                    na_out(a - 3)
            na_inv(15)
            for a in (13, 14, 15):
                na_out(a)

            def spread(k, sec):
                for j in range(16):
                    n = 16 * k + j
                    if n >= 2:
                        dve.wait_ge(S("sp_mm"), n - 1)
                    v.tensor_scalar(diag[:, n % 2, :], ident[:, :], modL[:, 16 * sec + j:16 * sec + j + 1], 128.0, ALU.mult, ALU.mult)\
                        .then_inc(S("diag"), 1)
                    own("diag")
            spread(0, G1)
            for t in range(2):
                normed(11 + t, y2a[:, t, :], y2a[:, t, :], 128)
            planes(3, 256)
            dve.wait_ge(S("spread"), 4)

            def resid2(base, i):
                p = (U0["O"] + i) % 2
                dve.wait_ge(S("mm_half"), base * 2 + (2 * (U0["O"] + i) + 2))
                for t in range(2):
                    v.tensor_tensor(ptmp[:, t, 0:256], ps[2 * p + t][:, 0:UC], g1b[:, bass.ds(base * UC + UC * i, UC)], ALU.mult)\
                        .then_inc(S("gated2"), 1)
                    dve.wait_ge(S("gated2"), base * 2 + (2 * i + t + 1))
                    c = x1[:, t, bass.ds(base * UC + UC * i, UC)]
                    m = v.tensor_tensor(c, c, ptmp[:, t, 0:256], ALU.add)
                m.then_inc(S(f"gemm_free{p}"), 1)
            stream(dve, lo, "O", resid2)

            wait_evacs(dve, U0["O"] + 7)
            for t in range(2):
                normed(13 + t, xs2[:, t, :], x1[:, t, :], 128)
            planes(4, 256)
            spread(1, G2)

            def glu(base, i):
                u0 = U0["L"]
                p = (u0 + i) % 2
                if i == 0:
                    for h in range(2):
                        dve.wait_ge(S("cg_mid"), base + (h + 1))
                        v.scalar_tensor_tensor(cgt[:, h, 1:256], ps[2 * p + h][:, 0:255], cols[:, bass.ds(base + (V_FCW0 + h), 1)],
                                               cgt[:, h, 1:256], ALU.mult, ALU.add).then_inc(S("cg_left"), 1)
                    for h in range(2):
                        dve.wait_ge(S("cg_left"), base + (h + 1))
                        v.scalar_tensor_tensor(cgt[:, h, 0:255], ps[2 * p + h][:, 1:256], cols[:, bass.ds(base + (V_FCW2 + h), 1)],
                                               cgt[:, h, 0:255], ALU.mult, ALU.add).then_inc(S("cg_all"), 1)
                    dve.wait_ge(S("cg_all"), base + 2)
                    dve.sem_inc(S(f"gemm_free{p}"), 1)
                else:
                    dve.wait_ge(S("gelu"), halfof(base) + 1)
                    for h in range(2):
                        dve.wait_ge(S("mm_half"), base * 2 + (2 * (u0 + i) + h + 1))
                        m = v.tensor_tensor(actT[:, bass.ds(base * 256 + 256 * h, 256)], cgt[:, h, :], ps[2 * p + h][:, 0:256], ALU.mult)
                    m.then_inc(S(f"gemm_free{p}"), 1)
            stream(dve, lo, "L", glu)
            stream(dve, lo, "M0", none)
            stream(dve, lo, "M1", none, last=True)
            dve.wait_ge(S("spread"), 8)
            dve.wait_ge(S("mm_half"), 2 * (U0["M1"] + 11))
            for t in range(2):
                for c in range(2):
                    for nb in range(2):
                        w = slice(1024 * c + 512 * nb, 1024 * c + 512 * nb + 512)
                        chain(v.tensor_tensor(t512, ps[4 * c + 2 * t + nb][:, :], g2b[:, w], ALU.mult))
                        v.tensor_tensor(x1[:, t, w], x1[:, t, w], t512, ALU.add).then_inc(S("x3"), 1)
                        own("x3")
            dve.wait_ge(S("fg_in"), 16)
            for t in range(2):
                dve.wait_ge(S("rms_root"), 15 + t + 1)
                k = 15 + t
                chain(v.reciprocal(stat[:, 40 + k:41 + k], stat[:, 20 + k:21 + k]))
                v.scalar_tensor_tensor(x1[:, t, :], x1[:, t, :], stat[:, 40 + k:41 + k], fgb, ALU.mult, ALU.mult).then_inc(S("final"), 1)
                own("final")

        @block.tensor
        def _(pe):
            mm = nc.tensor.matmul

            def unit(kind, c0, u0, base, i, first=False, final=False):
                p = (u0 + i) % 2
                for h in range(2):
                    pe.wait_ge(S("split_lo"), base * 2 + (2 * (u0 + i) + h + 1))
                    if kind == "DN" and h == 0:
                        pe.wait_ge(S("dn_lo"), base + (u0 + i - U0["M0"] + 1))
                    if kind != "DN" and h == 0 and u0 + i >= 2:
                        pe.wait_ge(S(f"gemm_free{p}"), halfof(base) + (u0 + i - p) // 2)
                    if kind in ("Tx", "Tall", "T") or (kind == "K" and h == 0):
                        w = T if kind in ("Tall", "K") else 256
                        cc = slice(0, T) if kind in ("Tall", "K") else slice(c0, c0 + 256)
                        o = ps[2 * p + h][:, 0:w]
                        for kt in range(KT):
                            k = slice(128 * kt, 128 * kt + 128)
                            mm(o, whi[h][:, k], phi[:, kt, cc], start=kt == 0, stop=False)
                            mm(o, whi[h][:, k], plo[:, kt, cc], start=False, stop=False)
                            l = mm(o, wlo[h][:, k], phi[:, kt, cc], start=False, stop=kt == KT - 1)
                    elif kind == "K":
                        for t in range(2):
                            o = ps[2 * p + 1][:, 16 * t:16 * t + 16]
                            tt = slice(META + 128 * t, META + 128 * t + 128)
                            for kt in range(KT):
                                k = slice(16 * kt, 16 * kt + 16)
                                mm(o, phi[:, kt, tt], whi[h][:, k], start=kt == 0, stop=False)
                                mm(o, plo[:, kt, tt], whi[h][:, k], start=False, stop=False)
                                l = mm(o, phi[:, kt, tt], wlo[h][:, k], start=False, stop=kt == KT - 1)
                    elif kind == "DN":
                        for q in range(2):
                            for t in range(2):
                                for nb in range(2):
                                    o = ps[4 * c0 + 2 * t + nb][:, :]
                                    k = slice(1024 * q + 512 * nb, 1024 * q + 512 * nb + 512)
                                    xh = phi[:, 4 * p + 2 * h + q, 128 * t:128 * t + 128]
                                    xl = plo[:, 4 * p + 2 * h + q, 128 * t:128 * t + 128]
                                    st, en = first and h == 0 and q == 0, final and h == 1 and q == 1
                                    mm(o, xh, whi[h][:, k], start=st, stop=False)
                                    mm(o, xl, whi[h][:, k], start=False, stop=False)
                                    l = mm(o, xh, wlo[h][:, k], start=False, stop=en)
                    elif kind == "BR":
                        for b in range(2):
                            o = ps[2 * p + h][:, 256 * b:256 * b + 256]
                            for kt in range(8 * b, 8 * b + 8):
                                k = slice(128 * kt, 128 * kt + 128)
                                st, en = kt == 8 * b, kt == 8 * b + 7
                                mm(o, whi[h][:, k], phi[:, kt, 0:256], start=st, stop=False)
                                mm(o, whi[h][:, k], plo[:, kt, 0:256], start=False, stop=False)
                                l = mm(o, wlo[h][:, k], phi[:, kt, 0:256], start=False, stop=en)
                    else:
                        tiles = [(2 * p, slice(c0, c0 + 128)), (2 * p + 1, slice(c0 + 128, c0 + 256))]
                        if kind == "N3":
                            tiles.append((4 + p, slice(0, 128)))
                        for k8 in range(8):
                            kt = 8 * h + k8
                            k = slice(UC * k8, UC * k8 + UC)
                            for b, tt in tiles:
                                o = ps[b][:, 0:UC]
                                mm(o, phi[:, kt, tt], whi[h][:, k], start=kt == 0, stop=False)
                                mm(o, plo[:, kt, tt], whi[h][:, k], start=False, stop=False)
                                l = mm(o, phi[:, kt, tt], wlo[h][:, k], start=False, stop=kt == KT - 1)
                    l.then_inc(S("mm_half"), 1)

            def phase(name, c0):
                units(pe, NU[name], lambda b, i: unit(KIND[name], c0, U0[name], b, i))

            def down(name, c):
                def one(b, i, first=False, final=False):
                    unit("DN", c, U0[name], b, i, first, final)
                one(0, 0, first=True)
                with pe.Fori(0, 4) as j:
                    for i in range(2):
                        one(j * 2, i + 1)
                one(0, 9)
                one(0, 10, final=True)

            def reduce(sec):
                pe.wait_ge(S("ada_acc"), 16 * sec + 17)
                if sec:
                    pe.wait_ge(S("mod_set"), sec)
                for a, b in (((1, 5), (0, 4)) if sec < 2 else ((ACC[sec], 4),)):
                    for j in range(16):
                        l = mm(ps[b][:, j:j + 1], acc[a][:, 128 * j:128 * j + 128], small[:, 1:2], start=True, stop=True)
                l.then_inc(S("ada_red"), 1)

            def planes(s, srcs):
                for kt in range(KT):
                    if kt >= 4:
                        pe.wait_ge(S("pl_tmp"), 16 * s + kt - 3)
                    a = 0
                    for src, n in srcs(kt):
                        l = nc.tensor.transpose(ps[4 + kt % 4][:, a:a + n], src, ident[0:n, 0:n])
                        a += n
                    l.then_inc(S("pl_tp"), 1)

            pe.wait_ge(S("id_in"), 16)
            pe.wait_ge(S("vec_in"), 16 * 16)
            for t, (c0, n) in enumerate(VEC_TILES):
                nc.tensor.transpose(ps[4 + t][:, 0:n], vecs[0:n, t, :], ident[0:n, 0:n]).then_inc(S("vec_tp"), 1)
            pe.wait_ge(S("cols_set"), 4)
            pe.wait_ge(S("rows_normed"), 3)
            planes(0, lambda kt: [(xin[0:n, t, 128 * kt:128 * kt + 128], n) for t, n in ((0, META), (1, 128), (2, 128))])
            pe.wait_ge(S("pl_lo"), 16)
            phase("A", META)
            phase("K", META)
            phase("B", META)
            phase("C", META)

            wait_evacs(pe, U0["D0"] - 1)
            pe.wait_ge(S("rope_in"), 32)
            pe.wait_ge(S("mean1_set"), 1)
            sq = RA(1024, 2, 512)

            def turn(c):
                chunk, w, _, _, _, pm = rope_of(c)
                if c < NNORM:
                    pe.wait_ge(S("nk_normed"), c + 1)
                if c >= 2:
                    pe.wait_ge(S("nk_turned"), c - 1)
                mm(ps[6 + c % 2][:, 0:w], pm, chunk, start=True, stop=True).then_inc(S("nk_rot"), 1)
            for c in range(13):
                if c < NNORM:
                    w = rope_of(c)[1]
                    pe.wait_ge(S("nk_sq"), c + 1)
                    if c >= 2:
                        pe.wait_ge(S("nk_root"), c - 1)
                    mm(ps[4 + c % 2][:, 0:w], mean1[:, :], sq[:, c % 2, 0:w], start=True, stop=True).then_inc(S("nk_mean"), 1)
                if c >= 1:
                    turn(c - 1)
            turn(12)

            pe.wait_ge(S("nk_turned"), 13)
            for s in range(32):
                qt, h = s // 16, s % 16
                r = slice(64 * (h % 2), 64 * (h % 2) + 64)
                if s >= 4:
                    pe.wait_ge(S("ix_relu"), s - 3)
                qi = projA[r, 256 * (h // 2) + 128 * qt:256 * (h // 2) + 128 * qt + 128]
                mm(ps[4 + s % 4][:, 0:T], qi, kiT[r, :], start=True, stop=True).then_inc(S("ix_mm"), 1)

            pe.wait_ge(S("ix_relu"), 32)
            L = RA(3072, 2, T)
            P = RA(3072 + 544, 2, T)
            PT = RA(4224, 2, 384)

            def qk(a):
                qt, h = a // 8, a % 8
                if a >= 2:
                    pe.wait_ge(S("at_max"), a - 1)
                qa = projA[:, 2048 + 256 * h + 128 * qt:2048 + 256 * h + 128 * qt + 128]
                mm(ps[4 + a % 2][:, 0:T], qa, projB[:, T * (h // 2):T * (h // 2) + T], start=True, stop=True).then_inc(S("at_qk"), 1)
            def pv(a):
                h = a % 8
                pe.wait_ge(S("at_pt"), a + 1)
                if a >= 2:
                    pe.wait_ge(S("att_out"), a - 1)
                g = slice(128 * (h // 2), 128 * (h // 2) + 128)
                o = ps[a % 2][:, 0:128]
                mm(o, projC[0:META, 0, g], PT[0:META, a % 2, 0:128], start=True, stop=False)
                mm(o, projC[:, 1, g], PT[:, a % 2, 128:256], start=False, stop=False)
                mm(o, projC[:, 2, g], PT[:, a % 2, 256:384], start=False, stop=True).then_inc(S("at_pv"), 1)
            qk(0)
            for a in range(16):
                if a + 1 < 16:
                    qk(a + 1)
                pe.wait_ge(S("at_norm"), a + 1)
                if a >= 2:
                    pe.wait_ge(S("at_pt"), a - 1)
                b = 6 + a % 2
                nc.tensor.transpose(ps[b][0:META, 0:128], P[:, a % 2, 0:META], ident[:, :])
                nc.tensor.transpose(ps[b][:, 128:256], P[:, a % 2, META:144], ident[:, :])
                nc.tensor.transpose(ps[b][:, 256:384], P[:, a % 2, 144:T], ident[:, :]).then_inc(S("at_tp"), 1)
                if a >= 1:
                    pv(a - 1)
            pv(15)

            pe.wait_ge(S("att_out"), 16)
            Qt, Kt, attn = RA(0, 2048), RA(2048, 2048), RA(4096, 2048)
            q = projA[:, 4096:6144]
            f = projB[:, 4 * T:12 * T]
            pe.wait_ge(S("hg_q"), 1)
            for l in range(8):
                if l < 7:
                    pe.wait_ge(S("lv_qk"), l + 1)
                for g in range(4):
                    if l >= 1:
                        pe.wait_ge(S("lv_sel"), 4 * (l - 1) + g + 1)
                    c, h0 = g % 2, 4 * (g // 2)
                    for h in range(h0, h0 + 4):
                        w = slice(256 * h + 128 * c, 256 * h + 128 * c + 128)
                        kk = Kt[:, w] if l < 7 else f[:, T * h + META + 128 * c:T * h + META + 128 * c + 128]
                        qq = Qt[:, w] if l < 7 else q[:, w]
                        x = mm(ps[4 + g][:, 128 * (h - h0):128 * (h - h0) + 128], kk, qq, start=True, stop=True)
                    x.then_inc(S("lv_mm"), 1)
            KD = RA(2048, 8, 144)
            KDT = R(2176, 2, 256)
            pe.wait_ge(S("kd"), 1)
            pe.wait_ge(S("lv_sel"), 32)

            def kdt(h):
                if h >= 2:
                    pe.wait_ge(S("kd_t"), h - 1)
                nc.tensor.transpose(ps[4 + h % 2][0:META, 0:128], KD[:, h, 0:META], ident[:, :])
                nc.tensor.transpose(ps[4 + h % 2][:, 128:256], KD[:, h, META:144], ident[:, :]).then_inc(S("kd_tp"), 1)
            kdt(0)
            for h in range(8):
                if h + 1 < 8:
                    kdt(h + 1)
                pe.wait_ge(S("kd_t"), h + 1)
                if h >= 2:
                    pe.wait_ge(S("state"), h - 1)
                vb = slice(512 + 128 * h, 512 + 128 * h + 128)
                mm(ps[6 + h % 2][:, 0:128], KDT[0:META, h % 2, 0:128], projC[0:META, 0, vb], start=True, stop=True)
                mm(ps[6 + h % 2][:, 128:256], KDT[:, h % 2, 128:256], projC[:, 1, vb], start=True, stop=True).then_inc(S("kd_mm"), 1)
            S2, S1 = R(2688, 8, 128), R(18960, 8, 128)
            pe.wait_ge(S("state"), 8)
            pe.wait_ge(S("q_in"), 1)
            for g in range(4):
                for h in (2 * g, 2 * g + 1):
                    for c in range(2):
                        vb = slice(512 + 128 * h, 512 + 128 * h + 128)
                        o = ps[4 + g][:, 256 * (h % 2) + 128 * c:256 * (h % 2) + 128 * c + 128]
                        ga = c + 2 * (h // 4)
                        mm(o, projC[:, 1 + c, vb], attn[:, 512 * ga + 128 * (h % 4):512 * ga + 128 * (h % 4) + 128], start=True, stop=False)
                        mm(o, (S2 if c else S1)[:, h, :], Qt[:, 256 * h + 128 * c:256 * h + 128 * c + 128], start=False, stop=True)\
                            .then_inc(S("hg_mm"), 1)
            for g in range(4):
                pe.wait_ge(S("hg_sq"), g + 1)
                mm(ps[4 + g][:, :], mean1[:, :], RA(512 * g, 512), start=True, stop=True).then_inc(S("hg_mean"), 1)

            for sec, ph in enumerate(("D0", "D1", "D2")):
                phase(ph, META)
                reduce(sec)
            pe.wait_ge(S("cp_lo"), 4)
            phase("E", 0)
            reduce(3)
            pe.wait_ge(S("cp_lo"), 8)
            phase("F", 0)
            reduce(4)

            def rows(src):
                return lambda kt: [(src[:, t, 128 * kt:128 * kt + 128], 128) for t in range(2)]
            pe.wait_ge(S("rows_normed"), 5)
            pe.wait_ge(S("mod_set"), 5)
            planes(1, rows(ctxr))
            pe.wait_ge(S("pl_lo"), 32)
            phase("G", 0)
            phase("H", 0)
            reduce(5)

            pe.wait_ge(S("rows_normed"), 7)
            pe.wait_ge(S("mod_set"), 6)
            planes(2, rows(xs1))
            pe.wait_ge(S("pl_lo"), 48)
            phase("I1", 0)
            for j in range(12):
                pe.wait_ge(S("cv_all"), j + 1)
                if j >= 4:
                    pe.wait_ge(S("hy_tok"), j - 3)
                nc.tensor.transpose(ps[4 + j % 4][:, 0:128], cv[:, j % 2, 0:128], ident[:, :])
                nc.tensor.transpose(ps[4 + j % 4][:, 128:256], cv[:, j % 2, 128:256], ident[:, :]).then_inc(S("hy_tp"), 1)
            pe.wait_ge(S("fh_in"), 16 * 12)
            pe.wait_ge(S("hy_tok"), 12)
            for g in range(4):
                for t in range(2):
                    n = 2 * g + t
                    if n >= 4:
                        pe.wait_ge(S("fd_ab"), n - 3)
                    mm(ps[4 + n % 4][:, 0:256], fhT[:, 256 * g + 128 * t:256 * g + 128 * t + 128], kcd, start=True, stop=True).then_inc(S("fd_mm"), 1)
            pe.wait_ge(S("fd_ab"), 8)
            for t in range(2):
                for kt in range(2):
                    for c in range(2):
                        l = mm(ps[4 + t][:, :], kCS[:, 2 * c + kt, 128 * t:128 * t + 128], AB[:, 2 * kt + c, :],
                               start=kt + c == 0, stop=kt + c == 2)
                l.then_inc(S("fl_mm"), 1)
            pe.wait_ge(S("fl_out"), 2)
            mm(ps[4][0:64, 0:256], w12[0:33, 0:64], kz[0:33, 0:256], start=True, stop=True).then_inc(S("fm_mm"), 1)
            pe.wait_ge(S("sin"), 1)
            mm(ps[5][0:64, 0:256], w12[0:64, 64:128], hid0[0:64, :], start=True, stop=True).then_inc(S("fm_mm"), 1)
            pe.wait_ge(S("sin"), 2)
            for o in range(2):
                if o:
                    pe.wait_ge(S("z1"), 2)
                for t in range(2):
                    for d in range(2):
                        c = 512 * (2 * o + d)
                        l = mm(ps[4 + 2 * t + d][:, :], hid[0:64, 128 * t:128 * t + 128], w3[0:64, c:c + 512], start=True, stop=True)
                    l.then_inc(S("fil_mm"), 1)
                pe.wait_ge(S("fil"), 2 * o + 2)
                for m in range(4):
                    for kt in range(2):
                        l = mm(ps[4 + m][:, :], kF[:, kt, 128 * m:128 * m + 128], hfil[:, kt + (2 if m >= 2 else 0), :], start=kt == 0, stop=kt == 1)
                l.then_inc(S("ks_mm"), 1)
                pe.wait_ge(S("ksp"), 2 * o + 1)
                for kt in range(2):
                    l = mm(ps[4][0:1, :], kF[:, kt, 256:257], hfil[:, kt, :], start=kt == 0, stop=kt == 1)
                l.then_inc(S("ks_mm"), 1)
                pe.wait_ge(S("ksp"), 2 * o + 2)
                for m in range(4):
                    for kt in range(2):
                        l = mm(ps[4 + m][:, :], kF[:, kt, 128 * m:128 * m + 128], u_tok[:, kt, 0:512], start=kt == 0, stop=kt == 1)
                l.then_inc(S("zs_mm"), 1)
                pe.wait_ge(S("ys"), 2 * o + 2)
                for t in range(2):
                    for m in range(4):
                        l = mm(ps[4 + t][:, :], kG[:, m, 128 * t:128 * t + 128], Yt[:, m, :], start=m == 0, stop=m == 3)
                    l.then_inc(S("yt_mm"), 1)

            pe.wait_ge(S("hy_out"), 2)
            phase("I2", 0)
            phase("J", 0)
            wait_evacs(pe, U0["O"] - 1)

            def qk2(a):
                qt, h = a // 8, a % 8
                if a >= 2:
                    pe.wait_ge(S("na_max"), a - 1)
                q2 = qkT[:, 256 * h + 128 * qt:256 * h + 128 * qt + 128]
                mm(ps[4 + a % 2][:, 0:256], q2, qkT[:, 2048 + 256 * h:2304 + 256 * h], start=True, stop=True)
                mm(ps[4 + a % 2][:, 256:512], q2, kcT[:, 256 * h:256 * h + 256], start=True, stop=True).then_inc(S("na_qk"), 1)
            pe.wait_ge(S("rpb_in"), 16 * 18)
            for c in range(6):
                if c >= 4:
                    pe.wait_ge(S("bias_set"), c - 3)
                mm(ps[4 + c % 4][:, :], flip, Uraw[:, 8 * c:8 * c + 8, :], start=True, stop=True).then_inc(S("flipped"), 1)
            pe.wait_ge(S("bias_set"), 6)
            def pv2(a):
                h = a % 8
                pe.wait_ge(S("na_pt"), a + 1)
                if a >= 2:
                    pe.wait_ge(S("na_out"), a - 1)
                g = slice(128 * h, 128 * h + 128)
                for kt in range(4):
                    l = mm(ps[a % 2][:, 0:128], PT2[:, a % 2, 128 * kt:128 * kt + 128], (v2 if kt < 2 else vc)[:, kt % 2, g],
                           start=kt == 0, stop=kt == 3)
                l.then_inc(S("na_pv"), 1)
            qk2(0)
            for a in range(16):
                if a + 1 < 16:
                    qk2(a + 1)
                pe.wait_ge(S("na_exp"), a + 1)
                if a >= 2:
                    pe.wait_ge(S("na_pt"), a - 1)
                for kt in range(4):
                    l = nc.tensor.transpose(ps[6 + a % 2][:, 128 * kt:128 * kt + 128], P2[:, a % 2, 128 * kt:128 * kt + 128], ident[:, :])
                l.then_inc(S("na_tp"), 1)
                if a >= 1:
                    pv2(a - 1)
            pv2(15)

            def spread(k):
                for j in range(16):
                    pe.wait_ge(S("diag"), 16 * k + j + 1)
                    mm(ps[4 + j // 4][:, 128 * (j % 4):128 * (j % 4) + 128], mean1[:, :], diag[:, j % 2, :], start=True, stop=True)\
                        .then_inc(S("sp_mm"), 1)
            pe.wait_ge(S("na_out"), 16)
            spread(0)
            pe.wait_ge(S("spread"), 4)
            pe.wait_ge(S("rows_normed"), 13)
            planes(3, lambda kt: [((y2a if kt < 8 else y2fh)[:, t, 128 * (kt % 8):128 * (kt % 8) + 128], 128) for t in range(2)])
            pe.wait_ge(S("pl_lo"), 64)
            phase("O", 0)

            pe.wait_ge(S("rows_normed"), 15)
            planes(4, rows(xs2))
            pe.wait_ge(S("pl_lo"), 80)
            spread(1)
            phase("L", 0)
            wait_evacs(pe, U0["M0"] - 1)
            pe.wait_ge(S("spread"), 8)
            down("M0", 0)
            down("M1", 1)


def constants():
    f = np.float32
    K = {"k_id": np.eye(128, dtype=f)}
    perm = np.zeros((128, 2, 128), f)
    for m in range(16):
        perm[m + 16, 0, m] = -1
        perm[m, 0, m + 16] = 1
    for o in (0, 64):
        for m in range(8):
            perm[o + m + 8, 1, o + m] = -1
            perm[o + m, 1, o + m + 8] = 1
    K["k_perm"] = perm
    rope = np.zeros((128, 4, T), f)
    rope[:, 0] = rope[:, 2] = 1
    pos = np.arange(T, dtype=f)
    for b, rot, offs in ((0, 32, (0,)), (2, 16, (0, 64))):
        inv = np.power(f(500000.0), -np.arange(0, rot, 2, dtype=f) / f(rot)).astype(f)
        ang = (pos[:, None] * inv[None, :]).astype(f)
        c, s = np.cos(ang).T.astype(f), np.sin(ang).T.astype(f)
        for o in offs:
            for half in range(2):
                rope[o + half * rot // 2:o + (half + 1) * rot // 2, b] = c
                rope[o + half * rot // 2:o + (half + 1) * rot // 2, b + 1] = s
    K["k_rope"] = rope
    chunk = np.where(np.arange(T) < META, 0, 1 + (np.arange(T) - META) // 64)
    adm = np.where(chunk[None, :] <= chunk[META:, None], f(0), f(NEG)).astype(f)
    K["k_adm"] = np.ascontiguousarray(adm.reshape(2, 128, T).transpose(1, 0, 2))
    s, t = np.arange(128)[:, None], np.arange(128)[None, :]
    lvl = np.zeros((128, 8, 128), np.int32)
    for l in range(7):
        m = 64 >> l
        lvl[:, l] = (s // (2 * m) == t // (2 * m)) & (s // m % 2 == 0) & (t // m % 2 == 1)
    lvl[:, 7] = s == t
    K["k_lvl"] = lvl.reshape(128, 1024)
    rst = np.ones((128, T), f)
    rst[:, [0, META, META + 128]] = 0
    K["k_rst"] = rst
    t = np.arange(256)[:, None]
    k = np.arange(256)[None, :]
    c, s = np.cos(2 * np.pi * (t * k % 512) / 512), np.sin(2 * np.pi * (t * k % 512) / 512)
    s[:, 0] = np.cos(np.pi * t[:, 0])
    F = np.concatenate([c, s], 1)
    K["k_F"] = np.ascontiguousarray(F.reshape(2, 128, 512).transpose(1, 0, 2)).astype(f)
    G = 2 * F.T / 512
    G[0] /= 2
    G[256] /= 2
    K["k_G"] = np.ascontiguousarray(G.reshape(4, 128, 256).transpose(1, 0, 2)).astype(f)
    d = np.outer(np.arange(128), np.arange(128)) % 128 * (2 * np.pi / 128)
    K["k_cd"] = np.concatenate([np.cos(d), -np.sin(d)], 1).astype(f)
    d = np.outer(np.arange(256), np.arange(256)) % 256 * (2 * np.pi / 256)
    CS = np.stack([np.cos(d), np.sin(d)]) / np.sqrt(256 * 128)
    K["k_CS"] = np.ascontiguousarray(CS.reshape(4, 128, 256).transpose(1, 0, 2)).astype(f)
    L = 256
    pos = np.arange(L, dtype=f)[:, None]
    tt = pos / f(L - 1)
    bands = np.linspace(1e-4, 15, 16, dtype=f)
    ang = (bands * f(2.0 * np.pi / L) * pos).astype(f)
    z = np.concatenate([tt, np.cos(ang), -np.sin(ang)], -1).astype(f)
    kz = np.zeros((128, 260), f)
    kz[0:33, 0:256] = z.T
    kz[:, 256:258] = 1
    kz[0, 256] = 0
    K["k_z"] = kz
    deltas = np.linspace(np.log(1e-2) / 1.5, np.log(1e-2) / 0.3, 512, dtype=f)
    w = np.exp(-tt * np.abs(deltas)[None, :]).astype(f)
    K["k_win"] = np.ascontiguousarray(w.reshape(2, 128, 512).transpose(1, 0, 2))
    col = np.arange(64)
    start = np.clip(col - 8, 0, 48)
    ok = (col[None, :] >= start[:, None]) & (col[None, :] < start[:, None] + 16)
    flip = np.zeros((128, 128), f)
    flip[np.arange(128), np.arange(128) // 64 * 64 + 63 - np.arange(128) % 64] = 1
    K["k_flip"] = flip
    K["k_col"] = np.tile(np.where(ok, f(0), f(NEG)), (2, 1)).astype(f)
    return K


_INS = ["x", "meta_tokens", "hgrn_lb_logits", "norm_g", "w_in", "q_norm_g", "k_norm_g", "idx_k_norm_g",
        "hgrn_out_norm_g", "w_branch", "w_out", "c_2", "ctx_2", "c_ctx_2", "ada_w_2", "ada_b_2", "norm1_g_2",
        "norm2_g_2", "w_in_2", "na_rpb_2", "hy_conv_w_2", "hy_conv_b_2", "hy_w1_2", "hy_b1_2", "hy_w2_2", "hy_b2_2",
        "hy_w3_2", "hy_freq_2", "hy_bias_2", "mix_norm_g_2", "w_out_2", "ffn_w_up_2", "ffn_conv_w_2",
        "ffn_conv_b_2", "ffn_w_down_2", "final_norm_g_2"]


def kernel(**inputs):
    import numpy as _np
    import concourse.bacc as _bacc
    from concourse import mybir as _mybir
    from concourse.bass_utils import run_bass_kernel_spmd as _run
    nc = _bacc.Bacc("TRN2", target_bir_lowering=False, num_devices=1, dynamic_dma_scratch_size=2048)
    arrays, aps = {}, {}
    given = {n: _np.ascontiguousarray(inputs[n]) for n in _INS}
    given.update(constants())
    for n, a in given.items():
        arrays[n + "_dram"] = a
        aps[n] = nc.dram_tensor(n + "_dram", a.shape, _mybir.dt.from_np(a.dtype), kind="ExternalInput").ap()
    o = nc.dram_tensor("out_dram", (1, SEQ, D), _mybir.dt.float32, kind="ExternalOutput").ap()
    program(nc, aps, o)
    r = _run(nc, [arrays], core_ids=[0])
    return r.results[0]["out_dram"]
```
